# Optimizing a Trainium2 kernel written in Bass

```python
import jax, jax.numpy as jnp
from jax import lax
import numpy as np

D_MODEL = 1024
BATCH = 1
SEQ = 256
DEPTH = 2

N_HEADS = 16
HEAD_DIM = D_MODEL // N_HEADS
N_MIXERS = 2
GRID_W = 64
NA_ROWS = 8
NA_COLS = 16
DIL_GROUPS = ((128, 1), (512, 4), (2048, 16))
N_GROUPS = len(DIL_GROUPS)
BAND_BLOCK = 128
D_FF = -(-8 * D_MODEL // (3 * 256)) * 256
RMS_EPS = 1e-6
NEG_INF = -1e30
N_A_LAYERS = (DEPTH + 1) // 2
N_B_LAYERS = DEPTH // 2


def rms_norm(x, g):
    xf = x.astype(jnp.float32)
    y = xf * lax.rsqrt(jnp.mean(xf * xf, axis=-1, keepdims=True) + RMS_EPS)
    return (y * g.astype(jnp.float32)).astype(x.dtype)

def alibi_slopes(n):
    return 2.0 ** (-8.0 * jnp.arange(1, n + 1, dtype=jnp.float32) / n)

def swiglu(x, w_gate, w_up, w_down):
    return (jax.nn.silu(x @ w_gate) * (x @ w_up)) @ w_down

def neighbourhood_attention(x, w_qkv, w_o, rpb):
    b, s, _ = x.shape
    rows = s // GRID_W
    kh = min(NA_ROWS, rows)
    qkv = (x @ w_qkv).reshape(b, rows, GRID_W, 3, N_HEADS, HEAD_DIM)
    q, k, v = (jnp.transpose(qkv[:, :, :, i], (0, 3, 1, 2, 4)) for i in range(3))
    q = q * HEAD_DIM ** -0.5
    col = jnp.arange(GRID_W)
    col_start = jnp.clip(col - NA_COLS // 2, 0, GRID_W - NA_COLS)
    col_mask = (col[None, :] >= col_start[:, None]) & (col[None, :] < col_start[:, None] + NA_COLS)
    col_idx = jnp.clip(col[None, :] - col[:, None] + NA_COLS - 1, 0, 2 * NA_COLS - 2)
    rpb_cols = rpb.astype(jnp.float32)[:, :, col_idx]

    def row_block(i):
        rs = jnp.clip(i - kh // 2, 0, rows - kh)
        qi = lax.dynamic_index_in_dim(q, i, axis=2, keepdims=False)
        kr = lax.dynamic_slice_in_dim(k, rs, kh, axis=2)
        vr = lax.dynamic_slice_in_dim(v, rs, kh, axis=2)
        bias = lax.dynamic_slice_in_dim(rpb_cols, rs - i + NA_ROWS - 1, kh, axis=1)
        sc = jnp.einsum('bhqd,bhrkd->bhqrk', qi, kr).astype(jnp.float32)
        sc = sc + jnp.transpose(bias, (0, 2, 1, 3))[None]
        sc = jnp.where(col_mask[:, None, :], sc, NEG_INF)
        p = jax.nn.softmax(sc.reshape(b, N_HEADS, GRID_W, kh * GRID_W), axis=-1).reshape(sc.shape)
        return jnp.einsum('bhqrk,bhrkd->bhqd', p.astype(vr.dtype), vr)

    o = lax.map(row_block, jnp.arange(rows))
    o = jnp.transpose(o, (1, 0, 3, 2, 4)).reshape(b, s, D_MODEL)
    return o @ w_o

def banded_attention(q, k, v, radius, slope_dist):
    n, h, l, dh = q.shape
    nb = -(-l // BAND_BLOCK)
    lp = nb * BAND_BLOCK
    qb = jnp.pad(q, ((0, 0), (0, 0), (0, lp - l), (0, 0))).reshape(n, h, nb, BAND_BLOCK, dh)

    def key_blocks(t):
        tp = jnp.pad(t, ((0, 0), (0, 0), (radius, lp - l + BAND_BLOCK - radius), (0, 0)))
        tp = tp.reshape(n, h, nb + 1, BAND_BLOCK, dh)
        return jnp.concatenate([tp[:, :, :-1], tp[:, :, 1:]], axis=3)

    kb, vb = key_blocks(k), key_blocks(v)
    qi = jnp.arange(lp).reshape(nb, BAND_BLOCK)
    kj = jnp.arange(nb)[:, None] * BAND_BLOCK - radius + jnp.arange(2 * BAND_BLOCK)[None, :]
    dist = jnp.abs(qi[:, :, None] - kj[:, None, :])
    valid = (dist <= radius) & (kj[:, None, :] >= 0) & (kj[:, None, :] < l)
    sc = jnp.einsum('nhbqd,nhbkd->nhbqk', qb, kb).astype(jnp.float32)
    sc = sc - slope_dist[None, :, None, None, None] * dist.astype(jnp.float32)
    sc = jnp.where(valid, sc, NEG_INF)
    lse = jax.nn.logsumexp(sc, axis=-1)
    p = jnp.exp(sc - lse[..., None])
    o = jnp.einsum('nhbqk,nhbkd->nhbqd', p.astype(vb.dtype), vb)
    return o.reshape(n, h, lp, dh)[:, :, :l], lse.reshape(n, h, lp)[:, :, :l]

def dilated_attention(x, w_qkv, w_o):
    b, s, _ = x.shape
    qkv = (x @ w_qkv).reshape(b, s, N_GROUPS, 3, N_HEADS, HEAD_DIM)
    slopes = alibi_slopes(N_HEADS)
    outs, lses = [], []
    for g, (window, dil) in enumerate(DIL_GROUPS):
        radius = window // (2 * dil)
        l = s // dil

        def to_sub(t):
            t = jnp.transpose(t.reshape(b, l, dil, N_HEADS, HEAD_DIM), (0, 2, 3, 1, 4))
            return t.reshape(b * dil, N_HEADS, l, HEAD_DIM)

        q, k, v = (to_sub(qkv[:, :, g, i]) for i in range(3))
        o, lse = banded_attention(q * HEAD_DIM ** -0.5, k, v, radius, slopes * dil)
        o = jnp.transpose(o.reshape(b, dil, N_HEADS, l, HEAD_DIM), (0, 3, 1, 2, 4)).reshape(b, s, N_HEADS, HEAD_DIM)
        lse = jnp.transpose(lse.reshape(b, dil, N_HEADS, l), (0, 3, 1, 2)).reshape(b, s, N_HEADS)
        outs.append(o)
        lses.append(lse)
    alpha = jax.nn.softmax(jnp.stack(lses, axis=0), axis=0)
    o = jnp.einsum('gbsh,gbshd->bshd', alpha, jnp.stack(outs, axis=0).astype(jnp.float32)).astype(x.dtype)
    return o.reshape(b, s, D_MODEL) @ w_o

def first_inputs(seed: int = 0) -> dict:
    key = jax.random.key(seed)
    ks = jax.random.split(key, 14)
    d = D_MODEL

    def w(k, shape, fan_in):
        return jax.random.normal(k, shape, jnp.float32) * fan_in ** -0.5

    def gain(k):
        return 1.0 + 0.02 * jax.random.normal(k, (DEPTH, d), jnp.float32)

    return {
        "x": jax.random.normal(ks[0], (BATCH, SEQ, d), jnp.float32),
        "norm_mix_pre": gain(ks[1]),
        "norm_mix_post": gain(ks[2]),
        "norm_ffn_pre": gain(ks[3]),
        "norm_ffn_post": gain(ks[4]),
        "na_w_qkv": w(ks[5], (N_A_LAYERS, d, 3 * d), d),
        "na_w_o": w(ks[6], (N_A_LAYERS, d, d), d),
        "na_rpb": 0.5 * jax.random.normal(ks[7], (N_A_LAYERS, N_HEADS, 2 * NA_ROWS - 1, 2 * NA_COLS - 1), jnp.float32),
        "dil_w_qkv": w(ks[8], (N_B_LAYERS, d, N_GROUPS * 3 * d), d),
        "dil_w_o": w(ks[9], (N_B_LAYERS, d, d), d),
        "ffn_w_gate": w(ks[10], (DEPTH, d, D_FF), d),
        "ffn_w_up": w(ks[11], (DEPTH, d, D_FF), d),
        "ffn_w_down": w(ks[12], (DEPTH, D_FF, d), D_FF),
    }

def first_block(x, norm_mix_pre, norm_mix_post, norm_ffn_pre, norm_ffn_post, na_w_qkv, na_w_o, na_rpb,
              dil_w_qkv, dil_w_o, ffn_w_gate, ffn_w_up, ffn_w_down):
    for layer in range(DEPTH):
        j = layer // N_MIXERS
        h = rms_norm(x, norm_mix_pre[layer])
        if layer % N_MIXERS == 0:
            h = neighbourhood_attention(h, na_w_qkv[j], na_w_o[j], na_rpb[j])
        else:
            h = dilated_attention(h, dil_w_qkv[j], dil_w_o[j])
        x = x + rms_norm(h, norm_mix_post[layer])
        h = rms_norm(x, norm_ffn_pre[layer])
        x = x + rms_norm(swiglu(h, ffn_w_gate[layer], ffn_w_up[layer], ffn_w_down[layer]), norm_ffn_post[layer])
    return x


MEM_LEN = 256
EPS = 1e-6
N_NORMS = 8
D_FF_2 = 2816
RW_HEADS = 8
RW_HEAD_DIM = 64
RW_WIDTH = RW_HEADS * RW_HEAD_DIM
RW_DECAY_RANK = 64
RW_AAA_RANK = 64
RW_GATE_RANK = 128
RW_LN_EPS = 64e-5
RW_SIZES = (RW_WIDTH, RW_WIDTH, RW_WIDTH, RW_DECAY_RANK, RW_AAA_RANK, RW_GATE_RANK)
RW_IN = 3 * RW_WIDTH + RW_DECAY_RANK + RW_AAA_RANK + RW_GATE_RANK
RT_HEADS = 4
RT_KEY_DIM = 128
RT_VAL_DIM = 128
RT_WIDTH = RT_HEADS * RT_VAL_DIM
RT_CHUNK = 128
RT_ROPE_BASE = 10000.0
RT_SIZES = (RT_HEADS * RT_KEY_DIM, RT_HEADS * RT_KEY_DIM, RT_WIDTH, RT_WIDTH)
RT_IN = 2 * RT_HEADS * RT_KEY_DIM + 2 * RT_WIDTH
EV_IN = RW_IN + RT_IN
EV_OUT = RW_WIDTH + RT_WIDTH
DSA_HEADS = 8
DSA_HEAD_DIM = 64
DSA_WIDTH = DSA_HEADS * DSA_HEAD_DIM
DSA_Q_RANK = 256
DSA_KV_RANK = 128
IDX_HEADS = 8
IDX_DIM = 64
TOPK_MAX = 256
Q_BLOCK = 128
DSA_SIZES = (DSA_Q_RANK, DSA_KV_RANK, IDX_DIM, IDX_HEADS)
DSA_IN = DSA_Q_RANK + DSA_KV_RANK + IDX_DIM + IDX_HEADS
SC_WIDTH = 512
SC_KERNEL = 3
SC_SIZES = (SC_WIDTH, SC_WIDTH, SC_WIDTH)
SC_IN = 3 * SC_WIDTH
OD_IN = DSA_IN + SC_IN
OD_OUT = DSA_WIDTH + SC_WIDTH
XA_HEADS = 4
XA_HEAD_DIM = 128
XA_WIDTH = XA_HEADS * XA_HEAD_DIM


F32 = jnp.float32

def split_cols(t, sizes):
    out, start = [], 0
    for s in sizes:
        out.append(t[..., start:start + s])
        start += s
    return out

def rms_norm_2(x, g, eps=EPS):
    xf = x.astype(F32)
    y = xf * lax.rsqrt(jnp.mean(xf * xf, axis=-1, keepdims=True) + eps)
    return (y * g.astype(F32)).astype(x.dtype)

def group_norm_heads(x, g, b, eps):
    xf = x.astype(F32)
    mu = jnp.mean(xf, axis=-1, keepdims=True)
    var = jnp.mean(jnp.square(xf - mu), axis=-1, keepdims=True)
    y = ((xf - mu) * lax.rsqrt(var + eps)).reshape(*x.shape[:-2], -1)
    return y * g.astype(F32) + b.astype(F32)

def token_shift(p):
    return jnp.pad(p, ((0, 0), (1, 0), (0, 0)))[:, :-1]

def swiglu_2(x, w_gate, w_up, w_down):
    return (jax.nn.silu(x @ w_gate) * (x @ w_up)) @ w_down

def rotary(x, positions):
    half = x.shape[-1] // 2
    inv_freq = RT_ROPE_BASE ** (-jnp.arange(half, dtype=F32) / half)
    ang = positions.astype(F32)[:, None] * inv_freq[None, :]
    cos = jnp.cos(ang)[None, :, None, :]
    sin = jnp.sin(ang)[None, :, None, :]
    x1, x2 = x[..., :half].astype(F32), x[..., half:].astype(F32)
    return jnp.concatenate([x1 * cos - x2 * sin, x1 * sin + x2 * cos], axis=-1).astype(x.dtype)

def rwkv7_mix(p, mu, w0, w2, a0, a2, g2, k_k, k_a, r_k, ln_g, ln_b):
    b_, s_, _ = p.shape
    p = p + (token_shift(p) - p) * mu
    r, k, v, xw, xa, xg = split_cols(p, RW_SIZES)
    w = -jax.nn.softplus(-(w0 + jnp.tanh(xw) @ w2)) - 0.5
    decay = jnp.exp(-jnp.exp(w.astype(F32)))
    a = jax.nn.sigmoid(a0 + xa @ a2)
    g = jax.nn.sigmoid(xg) @ g2
    heads = lambda t: t.reshape(b_, s_, RW_HEADS, RW_HEAD_DIM)
    kk = heads(k * k_k).astype(F32)
    kk = kk / jnp.maximum(jnp.sqrt(jnp.sum(kk * kk, axis=-1, keepdims=True)), 1e-12)
    k = k * (1 + (a - 1) * k_a)
    rh, kh, vh, ah = heads(r), heads(k), heads(v), heads(a).astype(F32)
    xs = tuple(jnp.moveaxis(t.astype(F32), 1, 0) for t in (rh, heads(decay), kh, vh, -kk, kk * ah))

    def step(state, inp):
        r_t, w_t, k_t, v_t, a_t, b_t = inp
        sa = jnp.einsum('bhvk,bhk->bhv', state, a_t)
        state = (state * w_t[:, :, None, :] + sa[..., None] * b_t[:, :, None, :]
                 + v_t[..., None] * k_t[:, :, None, :])
        return state, jnp.einsum('bhvk,bhk->bhv', state, r_t)

    state0 = jnp.zeros((b_, RW_HEADS, RW_HEAD_DIM, RW_HEAD_DIM), F32)
    _, y = lax.scan(step, state0, xs)
    y = group_norm_heads(jnp.moveaxis(y, 0, 1), ln_g, ln_b, RW_LN_EPS)
    bonus = jnp.sum(rh * kh * r_k, axis=-1, keepdims=True) * vh
    y = (y + bonus.reshape(b_, s_, RW_WIDTH).astype(F32)) * g.astype(F32)
    return y.astype(p.dtype)

def retention_mix(p, positions, gn_g, gn_b):
    b_, s_, _ = p.shape
    q, k, v, g = split_cols(p, RT_SIZES)
    q = rotary(q.reshape(b_, s_, RT_HEADS, RT_KEY_DIM), positions)
    k = rotary(k.reshape(b_, s_, RT_HEADS, RT_KEY_DIM), positions) * (RT_KEY_DIM ** -0.5)
    v = v.reshape(b_, s_, RT_HEADS, RT_VAL_DIM)
    n_chunks = s_ // RT_CHUNK
    chunk = lambda t: t.reshape(b_, n_chunks, RT_CHUNK, *t.shape[2:]).astype(F32)
    qc, kc, vc = chunk(q), chunk(k), chunk(v)
    log_gamma = jnp.log1p(-jnp.exp2(-5.0 - jnp.arange(RT_HEADS, dtype=F32)))
    idx = jnp.arange(RT_CHUNK, dtype=F32)
    rel = idx[:, None] - idx[None, :]
    decay_mask = jnp.where(rel[None] >= 0,
                           jnp.exp(jnp.maximum(rel, 0.0)[None] * log_gamma[:, None, None]), 0.0)
    scores = jnp.einsum('bnihd,bnjhd->bnhij', qc, kc) * decay_mask
    o_inner = jnp.einsum('bnhij,bnjhe->bnihe', scores, vc)
    zeta = jnp.exp((RT_CHUNK - 1 - idx)[None, :] * log_gamma[:, None])
    kv = jnp.einsum('bnjhd,hj,bnjhe->bnhde', kc, zeta, vc)
    chunk_gamma = jnp.exp(RT_CHUNK * log_gamma)[None, :, None, None]

    def step(state, kv_n):
        return state * chunk_gamma + kv_n, state

    state0 = jnp.zeros((b_, RT_HEADS, RT_KEY_DIM, RT_VAL_DIM), F32)
    _, r_prev = lax.scan(step, state0, jnp.moveaxis(kv, 1, 0))
    r_prev = jnp.moveaxis(r_prev, 0, 1)
    xi = jnp.exp((idx + 1)[:, None] * log_gamma[None, :])
    o_cross = jnp.einsum('bnihd,bnhde->bnihe', qc, r_prev) * xi[:, :, None]
    o = (o_inner + o_cross).reshape(b_, s_, RT_HEADS, RT_VAL_DIM)
    o = group_norm_heads(o, gn_g, gn_b, EPS)
    return (jax.nn.silu(g.astype(F32)) * o).astype(p.dtype)

def dsa_mix(p, q_norm_g, kv_norm_g, w_uq, w_uk, w_uv, w_qi):
    b_, s_, _ = p.shape
    c_q, c_kv, k_idx, w_idx = split_cols(p, DSA_SIZES)
    c_q = rms_norm_2(c_q, q_norm_g)
    c_kv = rms_norm_2(c_kv, kv_norm_g)
    q = jnp.einsum('btr,rhd->bthd', c_q, w_uq)
    q_lat = jnp.einsum('bthd,hdc->bthc', q, w_uk)
    q_idx = jnp.einsum('btr,rhd->bthd', c_q, w_qi)
    w_idx = w_idx * ((IDX_HEADS * IDX_DIM) ** -0.5)
    top_k = min(TOPK_MAX, s_ // 4)
    n_blocks = s_ // Q_BLOCK
    key_pos = jnp.arange(s_)

    def to_blocks(t):
        return jnp.moveaxis(t.reshape(b_, n_blocks, Q_BLOCK, *t.shape[2:]), 1, 0)

    def block(args):
        blk, ql, qi, wi = args
        q_pos = blk * Q_BLOCK + jnp.arange(Q_BLOCK)
        logits = jnp.einsum('bthd,bsd->bths', qi, k_idx)
        score = jnp.einsum('bth,bths->bts', wi, jax.nn.relu(logits)).astype(F32)
        causal = key_pos[None, :] <= q_pos[:, None]
        score = jnp.where(causal[None], score, -jnp.inf)
        top_val, top_idx = lax.top_k(score, top_k)
        valid = jnp.isfinite(top_val)
        sel = jax.vmap(lambda c, i: c[i])(c_kv, top_idx)
        s = jnp.einsum('bthc,btkc->bthk', ql, sel).astype(F32) * (DSA_HEAD_DIM ** -0.5)
        s = jnp.where(valid[:, :, None, :], s, -jnp.inf)
        prob = jax.nn.softmax(s, axis=-1).astype(sel.dtype)
        return jnp.einsum('bthk,btkc->bthc', prob, sel)

    o_lat = lax.map(block, (jnp.arange(n_blocks), to_blocks(q_lat), to_blocks(q_idx), to_blocks(w_idx)))
    o_lat = jnp.moveaxis(o_lat, 0, 1).reshape(b_, s_, DSA_HEADS, DSA_KV_RANK)
    o = jnp.einsum('bthc,hcd->bthd', o_lat, w_uv)
    return o.reshape(b_, s_, DSA_WIDTH).astype(p.dtype)

def short_conv_mix(p, conv_w, conv_b):
    h, gate_b, gate_c = split_cols(p, SC_SIZES)
    u = gate_c * h
    y = lax.conv_general_dilated(u, conv_w[:, None, :].astype(u.dtype), window_strides=(1,),
                                 padding=[(SC_KERNEL - 1, 0)],
                                 dimension_numbers=('NWC', 'WIO', 'NWC'),
                                 feature_group_count=SC_WIDTH) + conv_b
    return (gate_b * y).astype(p.dtype)

def memory_xattn(h, mem_n, wq, wk, wv, wo):
    b_, s_, _ = h.shape
    m_ = mem_n.shape[1]
    q = (h @ wq).reshape(b_, s_, XA_HEADS, XA_HEAD_DIM)
    k = (mem_n @ wk).reshape(b_, m_, XA_HEADS, XA_HEAD_DIM)
    v = (mem_n @ wv).reshape(b_, m_, XA_HEADS, XA_HEAD_DIM)
    s = jnp.einsum('bthd,bmhd->bhtm', q, k).astype(F32) * (XA_HEAD_DIM ** -0.5)
    prob = jax.nn.softmax(s, axis=-1).astype(v.dtype)
    o = jnp.einsum('bhtm,bmhd->bthd', prob, v).reshape(b_, s_, XA_WIDTH)
    return o @ wo

def second_inputs(seed: int = 0) -> dict:
    key = jax.random.key(seed)
    ks = iter(jax.random.split(key, 48))
    n_even = (DEPTH + 1) // 2
    n_odd = DEPTH // 2
    nrm = lambda shape, scale: jax.random.normal(next(ks), shape, F32) * scale
    gain = lambda shape: 1.0 + nrm(shape, 0.02)
    uni = lambda shape, lo, hi: jax.random.uniform(next(ks), shape, F32, lo, hi)
    return {
        'x': nrm((BATCH, SEQ, D_MODEL), 1.0),
        'mem': nrm((BATCH, MEM_LEN, D_MODEL), 1.0),
        'norm_g': gain((DEPTH, N_NORMS, D_MODEL)),
        'mem_norm_g': gain((D_MODEL,)),
        'ffn_w_gate': nrm((DEPTH, 2, D_MODEL, D_FF_2), D_MODEL ** -0.5),
        'ffn_w_up': nrm((DEPTH, 2, D_MODEL, D_FF_2), D_MODEL ** -0.5),
        'ffn_w_down': nrm((DEPTH, 2, D_FF_2, D_MODEL), D_FF_2 ** -0.5),
        'xa_wq': nrm((DEPTH, D_MODEL, XA_WIDTH), D_MODEL ** -0.5),
        'xa_wk': nrm((DEPTH, D_MODEL, XA_WIDTH), D_MODEL ** -0.5),
        'xa_wv': nrm((DEPTH, D_MODEL, XA_WIDTH), D_MODEL ** -0.5),
        'xa_wo': nrm((DEPTH, XA_WIDTH, D_MODEL), XA_WIDTH ** -0.5),
        'ev_w_in': nrm((n_even, D_MODEL, EV_IN), D_MODEL ** -0.5),
        'ev_w_out': nrm((n_even, EV_OUT, D_MODEL), EV_OUT ** -0.5),
        'rw_mu': uni((n_even, RW_IN), 0.0, 1.0),
        'rw_w0': uni((n_even, RW_WIDTH), -6.0, 1.0),
        'rw_w2': nrm((n_even, RW_DECAY_RANK, RW_WIDTH), 0.5 * RW_DECAY_RANK ** -0.5),
        'rw_a0': nrm((n_even, RW_WIDTH), 0.1),
        'rw_a2': nrm((n_even, RW_AAA_RANK, RW_WIDTH), 0.5 * RW_AAA_RANK ** -0.5),
        'rw_g2': nrm((n_even, RW_GATE_RANK, RW_WIDTH), RW_GATE_RANK ** -0.5),
        'rw_k_k': 0.85 + nrm((n_even, RW_WIDTH), 0.05),
        'rw_k_a': 1.0 + nrm((n_even, RW_WIDTH), 0.05),
        'rw_r_k': nrm((n_even, RW_HEADS, RW_HEAD_DIM), 0.1),
        'rw_ln_g': gain((n_even, RW_WIDTH)),
        'rw_ln_b': nrm((n_even, RW_WIDTH), 0.02),
        'rt_gn_g': gain((n_even, RT_WIDTH)),
        'rt_gn_b': nrm((n_even, RT_WIDTH), 0.02),
        'od_w_in': nrm((n_odd, D_MODEL, OD_IN), D_MODEL ** -0.5),
        'od_w_out': nrm((n_odd, OD_OUT, D_MODEL), OD_OUT ** -0.5),
        'dsa_q_norm_g': gain((n_odd, DSA_Q_RANK)),
        'dsa_kv_norm_g': gain((n_odd, DSA_KV_RANK)),
        'dsa_w_uq': nrm((n_odd, DSA_Q_RANK, DSA_HEADS, DSA_HEAD_DIM), DSA_Q_RANK ** -0.5),
        'dsa_w_uk': nrm((n_odd, DSA_HEADS, DSA_HEAD_DIM, DSA_KV_RANK), DSA_HEAD_DIM ** -0.5),
        'dsa_w_uv': nrm((n_odd, DSA_HEADS, DSA_KV_RANK, DSA_HEAD_DIM), DSA_KV_RANK ** -0.5),
        'dsa_w_qi': nrm((n_odd, DSA_Q_RANK, IDX_HEADS, IDX_DIM), DSA_Q_RANK ** -0.5),
        'sc_conv_w': nrm((n_odd, SC_KERNEL, SC_WIDTH), SC_KERNEL ** -0.5),
        'sc_conv_b': nrm((n_odd, SC_WIDTH), 0.02),
    }

def second_block(x, mem, norm_g, mem_norm_g, ffn_w_gate, ffn_w_up, ffn_w_down,
              xa_wq, xa_wk, xa_wv, xa_wo, ev_w_in, ev_w_out,
              rw_mu, rw_w0, rw_w2, rw_a0, rw_a2, rw_g2, rw_k_k, rw_k_a, rw_r_k, rw_ln_g, rw_ln_b,
              rt_gn_g, rt_gn_b, od_w_in, od_w_out,
              dsa_q_norm_g, dsa_kv_norm_g, dsa_w_uq, dsa_w_uk, dsa_w_uv, dsa_w_qi,
              sc_conv_w, sc_conv_b):
    mem_n = rms_norm_2(mem, mem_norm_g)
    positions = jnp.arange(x.shape[1])
    for l in range(DEPTH):
        ng = norm_g[l]
        h = swiglu_2(rms_norm_2(x, ng[0]), ffn_w_gate[l, 0], ffn_w_up[l, 0], ffn_w_down[l, 0])
        x = x + 0.5 * rms_norm_2(h, ng[1])
        h = rms_norm_2(x, ng[2])
        i = l // 2
        if l % 2 == 0:
            p = h @ ev_w_in[i]
            y_a = rwkv7_mix(p[..., :RW_IN], rw_mu[i], rw_w0[i], rw_w2[i], rw_a0[i], rw_a2[i],
                            rw_g2[i], rw_k_k[i], rw_k_a[i], rw_r_k[i], rw_ln_g[i], rw_ln_b[i])
            y_b = retention_mix(p[..., RW_IN:], positions, rt_gn_g[i], rt_gn_b[i])
            h = jnp.concatenate([y_a, y_b], axis=-1) @ ev_w_out[i]
        else:
            p = h @ od_w_in[i]
            y_c = dsa_mix(p[..., :DSA_IN], dsa_q_norm_g[i], dsa_kv_norm_g[i], dsa_w_uq[i],
                          dsa_w_uk[i], dsa_w_uv[i], dsa_w_qi[i])
            y_d = short_conv_mix(p[..., DSA_IN:], sc_conv_w[i], sc_conv_b[i])
            h = jnp.concatenate([y_c, y_d], axis=-1) @ od_w_out[i]
        x = x + rms_norm_2(h, ng[3])
        h = memory_xattn(rms_norm_2(x, ng[4]), mem_n, xa_wq[l], xa_wk[l], xa_wv[l], xa_wo[l])
        x = x + rms_norm_2(h, ng[5])
        h = swiglu_2(rms_norm_2(x, ng[6]), ffn_w_gate[l, 1], ffn_w_up[l, 1], ffn_w_down[l, 1])
        x = x + 0.5 * rms_norm_2(h, ng[7])
    return x


def setup_inputs(seed=0):
    out = dict(first_inputs(seed))
    for name, value in second_inputs(seed + 1).items():
        if name != "x":
            out[name + "_2"] = value
    return out


def reference(
    x, norm_mix_pre, norm_mix_post, norm_ffn_pre, norm_ffn_post, na_w_qkv, na_w_o, na_rpb,
    dil_w_qkv, dil_w_o, ffn_w_gate, ffn_w_up, ffn_w_down, mem_2, norm_g_2, mem_norm_g_2,
    ffn_w_gate_2, ffn_w_up_2, ffn_w_down_2, xa_wq_2, xa_wk_2, xa_wv_2, xa_wo_2, ev_w_in_2,
    ev_w_out_2, rw_mu_2, rw_w0_2, rw_w2_2, rw_a0_2, rw_a2_2, rw_g2_2, rw_k_k_2, rw_k_a_2,
    rw_r_k_2, rw_ln_g_2, rw_ln_b_2, rt_gn_g_2, rt_gn_b_2, od_w_in_2, od_w_out_2, dsa_q_norm_g_2,
    dsa_kv_norm_g_2, dsa_w_uq_2, dsa_w_uk_2, dsa_w_uv_2, dsa_w_qi_2, sc_conv_w_2, sc_conv_b_2,
):
    x = first_block(
        x, norm_mix_pre, norm_mix_post, norm_ffn_pre, norm_ffn_post, na_w_qkv, na_w_o, na_rpb,
        dil_w_qkv, dil_w_o, ffn_w_gate, ffn_w_up, ffn_w_down,
    )
    return second_block(
        x, mem_2, norm_g_2, mem_norm_g_2, ffn_w_gate_2, ffn_w_up_2, ffn_w_down_2, xa_wq_2,
        xa_wk_2, xa_wv_2, xa_wo_2, ev_w_in_2, ev_w_out_2, rw_mu_2, rw_w0_2, rw_w2_2, rw_a0_2,
        rw_a2_2, rw_g2_2, rw_k_k_2, rw_k_a_2, rw_r_k_2, rw_ln_g_2, rw_ln_b_2, rt_gn_g_2,
        rt_gn_b_2, od_w_in_2, od_w_out_2, dsa_q_norm_g_2, dsa_kv_norm_g_2, dsa_w_uq_2,
        dsa_w_uk_2, dsa_w_uv_2, dsa_w_qi_2, sc_conv_w_2, sc_conv_b_2,
    )


_drawn_inputs = setup_inputs


def setup_inputs(seed=0):
    import zlib

    import numpy as np

    out = dict(_drawn_inputs(seed))
    spreads = {}
    factors = {'mem_norm_g_2': 3.376,
     'rw_w2_2': 3.726,
     'rw_a0_2': 3.626,
     'rw_k_k_2': 2.827,
     'rw_ln_g_2': 6.831,
     'rw_ln_b_2': 6.542,
     'rt_gn_g_2': 6.495,
     'rt_gn_b_2': 6.355,
     'dsa_q_norm_g_2': 6.546,
     'dsa_kv_norm_g_2': 8.0,
     'sc_conv_b_2': 55.553}
    for name, (base, spread) in spreads.items():
        noise = np.random.default_rng([zlib.crc32(name.encode()), seed]).standard_normal(out[name].shape)
        drawn = base * np.exp(spread * noise) if base else spread * noise
        out[name] = __import__('jax').numpy.asarray(drawn.astype(out[name].dtype))
    for name, factor in factors.items():
        out[name] = (out[name] * factor).astype(out[name].dtype)
    return out
```

```python
from contextlib import ExitStack

import numpy as np

import concourse.bass as bass
from concourse import mybir

P = 128
D = 1024
T = 256
KT = D // P
FF = 2816
FT = FF // P
CHUNK = 2048
HEADS, HD = 16, 64
EPS = 1e-6

F32 = mybir.dt.float32
F32R = mybir.dt.float32r
I32 = mybir.dt.int32
ALU = mybir.AluOpType
ACT = mybir.ActivationFunctionType
AXX = mybir.AxisListType.X

STAGES = (
    ("na", 0), ("ffn", 0), ("dil", 0), ("ffn", 1),
    ("ffn", 2), ("rwrt", 0), ("xa", 0), ("ffn", 3),
    ("ffn", 4), ("dsa", 0), ("xa", 1), ("ffn", 5),
)
VECS = [(f"{s}{i}_{w}", KT) for s, i in STAGES for w in ("pre", "post")] + [
    ("mem_g", 8), ("mu", 14), ("w0", 4), ("a0", 4), ("k_k", 4), ("k_a", 4), ("r_k", 4), ("ln_g", 4), ("ln_b", 4),
    ("gn_g", 4), ("gn_b", 4), ("qn", 2), ("kvn", 1), ("cw0", 4), ("cw1", 4), ("cw2", 4), ("cb", 4),
]
VCOL = {}
NV = 0
for _n, _w in VECS:
    VCOL[_n] = NV
    NV += _w

RT_H = 4
CONSTS = [("ident", 128), ("ones", 128), ("blk", 128), ("swap", 128), ("slopes", 16), ("na_mask", 64),
          ("dist", 1024), ("rot_c", 256), ("rot_s", 256), ("decay", 2048), ("amask", 512), ("levels", 768),
          ("scan", 256), ("causal", 512)]
CCOL = {}
NC_ = 0
for _n, _w in CONSTS:
    CCOL[_n] = (NC_, _w)
    NC_ += _w


SMALLS = [("wa2", 512), ("g2", 512), ("uq", 1024), ("qi", 1024), ("uk", 512), ("uv", 512)]
SCOL = {}
SMALL_N = 0
for _n, _w in SMALLS:
    SCOL[_n] = (SMALL_N, _w)
    SMALL_N += _w


def small_parts(w):
    two = lambda a: a.reshape(2, P, 512).transpose(1, 0, 2).reshape(P, 1024)
    return {"wa2": np.concatenate([w["rw_w2_2"][0], w["rw_a2_2"][0]], axis=0), "g2": w["rw_g2_2"][0],
            "uq": two(w["dsa_w_uq_2"][0].reshape(256, 512)), "qi": two(w["dsa_w_qi_2"][0].reshape(256, 512)),
            "uk": w["dsa_w_uk_2"][0].reshape(4, P, P).transpose(1, 0, 2).reshape(P, 512),
            "uv": w["dsa_w_uv_2"][0].transpose(1, 0, 2).reshape(P, 512)}


def proj_chunks(kind):
    return {"na": 12, "ffn": FT, "dil": 36, "rwrt": 15, "xa": 6, "dsa": 9}[kind]


def out_tiles(kind):
    return {"na": 8, "ffn": FT, "dil": 8, "rwrt": 8, "xa": 4, "dsa": 8}[kind]


def n_chunks(stages):
    return sum(proj_chunks(k) + out_tiles(k) // 2 for k, _ in stages)


def build_program(nc, stages, wstream, xin, memin, vecs_d, consts_d, rpb, small, out):
    NCH = n_chunks(stages)
    with ExitStack() as ctx:
        def sb(name, shape, dt=F32):
            return ctx.enter_context(nc.sbuf_tensor(name, shape, dt))

        sems = {}

        def sem(name):
            if name not in sems:
                sems[name] = ctx.enter_context(nc.semaphore(name))
            return sems[name]

        NORM = {"sq": KT, "hi": KT, "lo": KT, "st": 1, "rs": 1, "bc": 1, "rb": 1}
        attn = lambda units, groups: {**{n: units for n in ("s", "sm", "p", "pn", "pt", "pts", "pv")}, "od": groups}
        ADDS = {"ffn": {n: FT for n in ("th", "a", "m", "hi2", "lo2")}, "na": {**attn(32, 8), "oh": 8},
                "dil": {**attn(32, 8), "oh": 8}, "xa": {**attn(8, 4), "oh": 4}, "dsa": attn(16, 8), "rwrt": {}}
        base, count = {}, {}

        def shares(tag, group, adds):
            for n, by in adds.items():
                base[tag, n] = (f"{group}_{n}", count.get((group, n), 0))
                count[group, n] = base[tag, n][1] + by

        for s_, (kind_, _) in enumerate(stages):
            shares(f"s{s_}pre", "pre", {**NORM, "x": KT if s_ else 0})
            shares(f"s{s_}", "ffn" if kind_ == "ffn" else "attn", ADDS[kind_])
            if kind_ == "xa":
                shares(f"s{s_}m", "mem", {**NORM, "n": KT, "ld": 16})
            shares(f"s{s_}post", "post", NORM)
        shares("end", "pre", {"x": KT})

        def sg(tag, n):
            return sem(base[tag, n][0] if (tag, n) in base else f"{tag}_{n}")

        def at(tag, n, value):
            return sg(tag, n), value + (base[tag, n][1] if (tag, n) in base else 0)

        xT = sb("xT", [P, KT, T])
        xh = sb("xh", [P, KT, T], F32R)
        xl = sb("xl", [P, KT, T], F32R)
        raw = sb("raw", [P, 3, CHUNK])
        whi = sb("whi", [P, 3, CHUNK], F32R)
        wlo = sb("wlo", [P, 3, CHUNK], F32R)
        vecs = sb("vecs", [P, NV])
        cst = sb("cst", [P, 3 * 128 + 16])
        rB = sb("rB", [P, T])
        rP = sb("rP", [P, T])
        rsc = sb("rsc", [P, 4])
        nt = sb("nt", [P, 16])
        sm = sb("sm", [P, 16])
        Sb = sb("Sb", [P, 2, 512])
        PTb = sb("PTb", [P, 2, 512])
        ar_at = -(-nc.sbuf_base // 64) * 64
        AR = nc.alloc_sbuf_tensor_at("AR", [P, 2 * FT, T], F32R, offset=ar_at)
        FS = (nc.sbuf_usable_end - ar_at - 16 * T * 4) // 4 // 16 * 16
        F0 = nc.alloc_sbuf_tensor_at("F0", [P, FS], F32, offset=ar_at + 16 * T * 4)
        ident = cst[:, 0:128]
        ones = cst[:, 128:256]
        blk = cst[:, 256:384]
        slopes = cst[:, 384:400]

        acc = [ctx.enter_context(nc.psum_tensor(f"acc{i}", [P, 512], F32)) for i in range(4)]
        pj = [ctx.enter_context(nc.psum_tensor(f"pj{i}", [P, 512], F32)) for i in range(3)]
        mb = ctx.enter_context(nc.psum_tensor("mb", [P, 512], F32))

        def v(name, k):
            return vecs[:, VCOL[name] + k:VCOL[name] + k + 1]

        def c_dram(name):
            a, n = CCOL[name]
            return consts_d[:, a:a + n]

        def arena():
            at = [0]

            def take(*shape):
                n = int(np.prod(shape))
                a = F0[:, at[0]:at[0] + n]
                at[0] += n
                assert at[0] <= FS, (at[0], FS)
                if len(shape) == 2:
                    a = a.rearrange("p (a b) -> p a b", b=shape[1])
                elif len(shape) == 3:
                    a = a.rearrange("p (a b c) -> p a b c", b=shape[1], c=shape[2])
                elif len(shape) == 4:
                    a = a.rearrange("p (a b c d) -> p a b c d", b=shape[1], c=shape[2], d=shape[3])
                return a
            return take

        w_raw = [sem(f"w_raw{j}") for j in range(3)]
        w_hi = sem("w_hi")
        w_lo = sem("w_lo")
        w_used = sem("w_used")
        pj_free = sem("pj_free")
        loaded = sem("loaded")
        vchain = sem("vchain")

        class Walk:
            def __init__(self):
                self.g = 0
                self.p = 0

        def chunk_loop(eng, w, n, body, peel=0, is_proj=False, last=False):
            g0, p0 = w.g, w.p
            for c in range(peel):
                body(c, g0 + c, (g0 + c) % 3, (g0 + c) // 3, p0 + c, (p0 + c) % 3)
            rest = n - peel
            q = max(0, (rest - 3) // 3) if last else rest // 3
            c0 = peel
            if q > 1:
                with eng.Fori(0, q) as i:
                    for j in range(3):
                        s = c0 + j
                        body(i * 3 + s, i * 3 + (g0 + s), (g0 + s) % 3, i + (g0 + s) // 3,
                             i * 3 + (p0 + s), (p0 + s) % 3)
                c0 += 3 * q
            for c in range(c0, n):
                body(c, g0 + c, (g0 + c) % 3, (g0 + c) // 3, p0 + c, (p0 + c) % 3)
            w.g += n
            if is_proj:
                w.p += n

        def mm3(o, slot, b, k_hi, k_lo, first, last, inc=None):
            wh = whi[:, slot, b * P:(b + 1) * P]
            wl = wlo[:, slot, b * P:(b + 1) * P]
            nc.tensor.matmul(o, wh, k_hi, start=first, stop=False, skip_group_check=True)
            nc.tensor.matmul(o, wh, k_lo, start=False, stop=False, skip_group_check=True)
            return nc.tensor.matmul(o, wl, k_hi, start=False, stop=last, skip_group_check=True)

        def mm3t(o, slot, b, k_hi, k_lo, first, last, n=P):
            wh = whi[:, slot, b * P:b * P + n]
            wl = wlo[:, slot, b * P:b * P + n]
            nc.tensor.matmul(o, k_hi, wh, start=first, stop=False, skip_group_check=True)
            nc.tensor.matmul(o, k_lo, wh, start=False, stop=False, skip_group_check=True)
            return nc.tensor.matmul(o, k_hi, wl, start=False, stop=last, skip_group_check=True)

        after_chunk = []
        split_tag = []

        def tile_fm(bank, half, slot, hs=xh, ls=xl, off=0, lofs=0):
            first_of = split_tag.pop() if split_tag else None
            for k in range(KT):
                if first_of:
                    nc.tensor.wait_ge(*at(first_of, "lo", k + 1))
                last = mm3(bank[:, half * T:(half + 1) * T], slot, half * KT + k, hs[:, off + k, :], ls[:, lofs + k, :],
                           k == 0, k == KT - 1)
            return last

        def tile_tm(bank, half, slot, hs=xh, ls=xl, n=P, off=0, lofs=0):
            for t in range(2):
                for k in range(KT):
                    last = mm3t(bank[:, half * T + t * P:half * T + t * P + n], slot, half * KT + k,
                                hs[:, off + k, t * P:(t + 1) * P], ls[:, lofs + k, t * P:(t + 1) * P],
                                k == 0, k == KT - 1, n)
            return last

        n_v = [0]

        def link(dve, ins):
            n_v[0] += 1
            ins.then_inc(vchain, 1)
            dve.wait_ge(vchain, n_v[0])

        def rsqrt(dve, y, x, n, tmp, tmi):
            link(dve, nc.vector.tensor_scalar(tmi.bitcast(I32), x.bitcast(I32), 1, None, ALU.logical_shift_right))
            link(dve, nc.vector.tensor_scalar(y.bitcast(I32), tmi.bitcast(I32), -1.0, float(0x5F3759DF),
                                              ALU.mult, ALU.add))
            for _ in range(3):
                link(dve, nc.vector.tensor_tensor(tmp, y, y, ALU.mult))
                link(dve, nc.vector.scalar_tensor_tensor(tmp, tmp, -0.5, x, ALU.mult, ALU.mult))
                link(dve, nc.vector.scalar_tensor_tensor(y, tmp, 1.5, y, ALU.add, ALU.mult))

        def act_hi(act, g, gs, it, c):
            if isinstance(g, int) and g + 3 >= NCH:
                return
            act.wait_ge(w_used, g + 1)
            act.wait_ge(w_raw[gs], (it + 2) * 16)
            nc.scalar.activation(whi[:, gs, :], raw[:, gs, :], ACT.Copy).then_inc(w_hi, 1)

        def act_phase(act, w, n, is_proj=False):
            chunk_loop(act, w, n, lambda c, g, gs, it, p, ps: act_hi(act, g, gs, it, c), is_proj=is_proj)

        SQoff = FS - KT * T
        SQ = F0[:, SQoff:SQoff + KT * T].rearrange("p (k t) -> p k t", t=T)

        def perm_view(a):
            return a.rearrange("p (r l) -> p l r", r=4)

        def natural(a):
            return a.rearrange("p (l r) -> p l r", r=4)

        def stats_pe(pe, tag, src=None, n=KT):
            src = SQ if src is None else src
            pe.wait_ge(*at(tag, "sq", n))
            for t in range(2):
                for k in range(n):
                    last = nc.tensor.matmul(mb[:, 510 + t:511 + t], src[:, k, t * P:(t + 1) * P], ones[:, 0:1],
                                            start=k == 0, stop=k == n - 1)
            last.then_inc(sg(tag, "st"), 1)

        def stats_dve(dve, tag, rs, scale, eps, post=1.0):
            dve.wait_ge(*at(tag, "st", 1))
            link(dve, nc.vector.tensor_scalar(nt[:, 0:2], mb[:, 510:512], scale, eps, ALU.mult, ALU.add))
            rsqrt(dve, rs, nt[:, 0:2], 2, nt[:, 2:4], nt[:, 4:6])
            if post != 1.0:
                link(dve, nc.vector.tensor_scalar(rs, rs, post, None, ALU.mult))
            nc.vector.tensor_copy(nt[:, 6:8], rs).then_inc(sg(tag, "rs"), 1)

        def bcast_pe(pe, tag, rs):
            pe.wait_ge(*at(tag, "rs", 1))
            for t in range(2):
                last = nc.tensor.matmul(mb[:, t * P:(t + 1) * P], rs[:, t:t + 1].to_broadcast([P, P]), ident,
                                        start=True, stop=True)
            last.then_inc(sg(tag, "bc"), 1)

        def bcast_dve(dve, tag, dst):
            dve.wait_ge(*at(tag, "bc", 1))
            nc.vector.tensor_copy(dst, mb[:, 0:T]).then_inc(sg(tag, "rb"), 1)
            dve.wait_ge(*at(tag, "rb", 1))

        def pre_act(act, tag, gain, perm):
            for k in range(KT):
                if tag != "s0pre":
                    act.wait_ge(*at(tag, "x", k + 1))
                src = xT[:, k, :]
                nc.scalar.activation(SQ[:, k, :] if not perm else perm_view(SQ[:, k, :]),
                                     src if not perm else natural(src), ACT.Square).then_inc(sg(tag, "sq"), 1)
                nc.scalar.activation(xh[:, k, :] if not perm else perm_view(xh[:, k, :]),
                                     src if not perm else natural(src), ACT.Copy,
                                     scale=v(gain, k)).then_inc(sg(tag, "hi"), 1)

        def pre_lo(dve, tag, gain, perm, k):
            dve.wait_ge(*at(tag, "hi", k + 1))
            f = (lambda a: a) if not perm else perm_view
            n = (lambda a: a) if not perm else natural
            nc.vector.scalar_tensor_tensor(f(xl[:, k, :]), n(xT[:, k, :]), v(gain, k), f(xh[:, k, :].bitcast(F32)),
                                           ALU.mult, ALU.subtract).then_inc(sg(tag, "lo"), 1)

        def pre_dve(dve, tag, gain, perm, done_lo=False):
            if not done_lo:
                for k in range(KT):
                    pre_lo(dve, tag, gain, perm, k)
            stats_dve(dve, tag, rsc[:, 2:4], 1.0 / D, EPS)
            bcast_dve(dve, tag, rP[:, :])

        def pre_pe(pe, tag):
            split_tag.append(tag)
            if tag == "s0pre":
                stats_pe(pe, tag)
                bcast_pe(pe, tag, rsc[:, 2:4])
                return
            after_chunk.append(lambda: stats_pe(pe, tag))
            after_chunk.append(lambda: bcast_pe(pe, tag, rsc[:, 2:4]))

        def post_act(act, w, tag):
            act.wait_ge(w_used, w.g)
            for b in range(4):
                nc.scalar.activation(SQ[:, 2 * b:2 * b + 2, :].rearrange("p k t -> p (k t)"), acc[b][:, :],
                                     ACT.Square).then_inc(sg(tag, "sq"), 2)

        def post_pe(pe, tag):
            stats_pe(pe, tag)
            bcast_pe(pe, tag, rsc[:, 0:2])

        def post_dve(dve, tag, gain, half, nxt):
            stats_dve(dve, tag, rsc[:, 0:2], 1.0 / D, EPS, half)
            bcast_dve(dve, tag, rB[:, :])
            for k in range(KT):
                tmp = Sb[:, k % 2, 0:T]
                link(dve, nc.vector.scalar_tensor_tensor(tmp, acc[k // 2][:, (k % 2) * T:(k % 2 + 1) * T],
                                                         v(gain, k), rB[:, :], ALU.mult, ALU.mult))
                nc.vector.tensor_tensor(xT[:, k, :], xT[:, k, :], tmp, ALU.add).then_inc(sg(nxt[0], "x"), 1)
                if nxt[1] and k > 0:
                    pre_lo(dve, nxt[0], nxt[1], nxt[2], k - 1)
            if nxt[1]:
                pre_lo(dve, nxt[0], nxt[1], nxt[2], KT - 1)

        def out_pe(pe, w, nk, lo_at, tag, ready):
            def body(c, g, gs, it, p, ps):
                pe.wait_ge(w_lo, g + 1)
                for kk in range(2):
                    pe.wait_ge(*at(tag, ready, c * 2 + kk + 1))
                    for n in range(8):
                        if isinstance(c, int):
                            kt = 2 * c + kk
                            ah, al = AR[:, kt, :], AR[:, lo_at + kt, :]
                            first, fin = kt == 0 and n % 2 == 0, kt == nk - 1
                        else:
                            ah = AR[:, bass.ds(c * 2 + kk, 1), :]
                            al = AR[:, bass.ds(c * 2 + (kk + lo_at), 1), :]
                            first = fin = False
                        x = mm3(acc[n // 2][:, (n % 2) * T:(n % 2 + 1) * T], gs, kk * 8 + n, ah, al, first, fin)
                x.then_inc(w_used, 1)
            n = nk // 2
            chunk_loop(pe, w, n, body, peel=1, last=True)

        def out_act(act, w, nk):
            chunk_loop(act, w, nk // 2, lambda c, g, gs, it, p, ps: act_hi(act, g, gs, it, c), peel=1, last=True)

        def proj_pe(pe, w, n, tiles):
            def body(c, g, gs, it, p, ps):
                pe.wait_ge(w_lo, g + 1)
                pe.wait_ge(pj_free, p + 1)
                j = c % 3 if isinstance(c, int) else None
                tiles(c, (gs - w.g) % 3, pj[ps], gs).then_inc(w_used, 1)
                if after_chunk:
                    after_chunk.pop(0)()
            chunk_loop(pe, w, n, body, peel=min(n, len(after_chunk)), is_proj=True)

        def attn_pe(pe, tag, units, u0, deep=2, after=lambda i: None):
            def scores(u, U):
                if u >= 2:
                    pe.wait_ge(*at(tag, "sm", u - 1))
                if "ready" in U:
                    pe.wait_ge(pj_free, 3 + U["ready"])
                b = acc[u % 2]
                for lhsT, rhs, c0, n in U["scores"]:
                    last = nc.tensor.matmul(b[:, c0:c0 + n], lhsT, rhs, start=True, stop=True)
                last.then_inc(sg(tag, "s"), 1)

            def transposes(u, U):
                pe.wait_ge(*at(tag, "pn", u + 1))
                if u >= 2:
                    pe.wait_ge(*at(tag, "pts", u - 1))
                for j in range(U["nk"] // P):
                    last = nc.tensor.transpose(acc[2 + u % 2][:, j * P:(j + 1) * P], Sb[:, u % 2, j * P:(j + 1) * P],
                                               ident)
                last.then_inc(sg(tag, "pt"), 1)

            def values(u, U):
                pe.wait_ge(*at(tag, "pts", u + 1))
                if U["grp"] >= deep:
                    pe.wait_ge(*at(tag, "od", U["grp"] + 1 - deep))
                n = len(U["pv"])
                for i, (va, c0) in enumerate(U["pv"]):
                    last = nc.tensor.matmul(U["out"], va, PTb[:, u % 2, c0:c0 + P], start=i == 0, stop=i == n - 1)
                last.then_inc(sg(tag, "pv"), 1)

            scores(u0, units[0])
            scores(u0 + 1, units[1])
            for i, U in enumerate(units):
                if i + 2 < len(units):
                    scores(u0 + i + 2, units[i + 2])
                transposes(u0 + i, U)
                if i:
                    values(u0 + i - 1, units[i - 1])
                after(i)
            values(u0 + len(units) - 1, units[-1])

        def attn_dve(dve, tag, units, u0, finish, after=lambda i: None, busy=()):
            def softmax_a(u, U):
                dve.wait_ge(*at(tag, "s", u + 1))
                if u >= 2:
                    dve.wait_ge(*at(tag, "pt", u - 1))
                S = Sb[:, u % 2, 0:U["nk"]]
                link(dve, U["soft"](S, acc[u % 2][:, 0:U["nk"]]))
                nc.vector.tensor_reduce(sm[:, u % 2:u % 2 + 1], S, AXX, ALU.max, negate=True)\
                    .then_inc(sg(tag, "sm"), 1)

            def softmax_b(u, U):
                dve.wait_ge(*at(tag, "p", u + 1))
                S = Sb[:, u % 2, 0:U["nk"]]
                r = sm[:, 4 + u % 2:5 + u % 2]
                link(dve, nc.vector.reciprocal(r, sm[:, 2 + u % 2:3 + u % 2]))
                nc.vector.tensor_scalar(S, S, r, None, ALU.mult).then_inc(sg(tag, "pn"), 1)

            softmax_a(u0, units[0])
            softmax_a(u0 + 1, units[1])
            for i, U in enumerate(units):
                if i - 1 not in busy:
                    softmax_b(u0 + i, U)
                if i + 2 < len(units):
                    softmax_a(u0 + i + 2, units[i + 2])
                if i and units[i - 1]["end"]:
                    finish(units[i - 1]["grp"])
                if i in busy and i + 1 < len(units):
                    softmax_b(u0 + i + 1, units[i + 1])
                after(i)
            finish(units[-1]["grp"])

        def attn_act(act, tag, units, u0, finish, after=lambda i: None):
            def exps(u, U):
                act.wait_ge(*at(tag, "sm", u + 1))
                S = Sb[:, u % 2, 0:U["nk"]]
                nc.scalar.activation(S, S, ACT.Exp, bias=sm[:, u % 2:u % 2 + 1],
                                     accum_out=sm[:, 2 + u % 2:3 + u % 2]).then_inc(sg(tag, "p"), 1)

            def copy_pt(u, U):
                act.wait_ge(*at(tag, "pt", u + 1))
                if u >= 2:
                    act.wait_ge(*at(tag, "pv", u - 1))
                n = U["nk"]
                nc.scalar.activation(PTb[:, u % 2, 0:n], acc[2 + u % 2][:, 0:n], ACT.Copy)\
                    .then_inc(sg(tag, "pts"), 1)

            def fin(u, U):
                act.wait_ge(*at(tag, "pv", u + 1))
                finish(U["grp"])

            exps(u0, units[0])
            exps(u0 + 1, units[1])
            for i, U in enumerate(units):
                copy_pt(u0 + i, U)
                if i and units[i - 1]["end"]:
                    fin(u0 + i - 1, units[i - 1])
                if i + 2 < len(units):
                    exps(u0 + i + 2, units[i + 2])
                after(i)
            fin(u0 + len(units) - 1, units[-1])

        def o_bank(grp):
            return (mb, pj[2])[grp % 2][:, 0:T]

        def split_out(tag, perm, o_bank=o_bank):
            def dst(a):
                return a if not perm else a.rearrange("p (l r) -> p r l", r=4)

            def src(a):
                return a if not perm else a.rearrange("p (r l) -> p r l", r=4)

            def hi(grp):
                nc.scalar.activation(dst(AR[:, grp, :]), src(o_bank(grp)), ACT.Copy).then_inc(sg(tag, "oh"), 1)

            def lo(dve):
                def f(grp):
                    dve.wait_ge(*at(tag, "oh", grp + 1))
                    nc.vector.tensor_tensor(dst(AR[:, 8 + grp, :]), src(o_bank(grp)),
                                            dst(AR[:, grp, :].bitcast(F32)), ALU.subtract)\
                        .then_inc(sg(tag, "od"), 1)
                return f
            return hi, lo


        def ffn(tag):
            sh = FS - KT * T - 5 * T
            GU = F0[:, sh:sh + 512]
            TH = F0[:, sh + 512:sh + 768]
            A = F0[:, sh + 768:sh + 1024]
            M = F0[:, sh + 1024:sh + 1280]

            def pe_f(pe, w):
                def tiles(c, j, bank, slot):
                    tile_fm(bank, 0, slot)
                    return tile_fm(bank, 1, slot)
                proj_pe(pe, w, FT, tiles)
                out_pe(pe, w, FT, FT, tag, "lo2")

            def dve_f(dve, w):
                def body(c, g, gs, it, p, ps):
                    dve.wait_ge(w_used, g + 1)
                    nc.vector.tensor_tensor(GU.rearrange("p (a t) -> p a t", a=2),
                                            pj[ps][:, :].rearrange("p (a t) -> p a t", a=2),
                                            rP[:, None, :].to_broadcast([P, 2, T]), ALU.mult).then_inc(pj_free, 1)
                    dve.wait_ge(*at(tag, "th", c + 1))
                    nc.vector.scalar_tensor_tensor(A, TH, 1.0, GU[:, 0:T], ALU.add, ALU.mult)\
                        .then_inc(sg(tag, "a"), 1)
                    dve.wait_ge(*at(tag, "a", c + 1))
                    nc.vector.scalar_tensor_tensor(M, A, 0.5, GU[:, T:2 * T], ALU.mult, ALU.mult)\
                        .then_inc(sg(tag, "m"), 1)
                    dve.wait_ge(*at(tag, "hi2", c + 1))
                    nc.vector.tensor_tensor(AR[:, bass.ds(c + FT, 1), :] if not isinstance(c, int) else AR[:, c + FT, :],
                                            M, (AR[:, bass.ds(c, 1), :] if not isinstance(c, int)
                                                else AR[:, c, :]).bitcast(F32),
                                            ALU.subtract).then_inc(sg(tag, "lo2"), 1)
                chunk_loop(dve, w, FT, body, is_proj=True)
                w.g += FT // 2

            def act_f(act, w):
                def body(c, g, gs, it, p, ps):
                    act_hi(act, g, gs, it, c)
                    act.wait_ge(pj_free, p + 4)
                    nc.scalar.activation(TH, GU[:, 0:T], ACT.Tanh, scale=0.5).then_inc(sg(tag, "th"), 1)
                    act.wait_ge(*at(tag, "m", c + 1))
                    nc.scalar.activation(AR[:, bass.ds(c, 1), :] if not isinstance(c, int) else AR[:, c, :],
                                         M, ACT.Copy).then_inc(sg(tag, "hi2"), 1)
                chunk_loop(act, w, FT, body, is_proj=True)
                out_act(act, w, FT)
            return pe_f, dve_f, act_f

        def mixer(tag, kind):
            take = arena()
            na = kind == "na"
            ntr = 2 if na else 6
            QBs, KBs, VBs = ([take(ntr, T) for _ in range(2)], [take(ntr, T) for _ in range(2)],
                             [take(ntr, 2, P) for _ in range(2)])
            if na:
                NB = take(2, HEADS, T)
                MK = take(64)
            else:
                DM = take(2, 512)
            one_bank = lambda grp: mb[:, 0:T]
            hi_f, lo_f = split_out(tag, not na, one_bank)
            NCP = 3 * ntr // 2

            def chunks_behind(u):
                ps_, i = divmod(u, 8)
                return range(NCP * i // 6, NCP * (i + 1) // 6) if ps_ < 3 and i < 6 else range(0)

            def all_units(p0):
                us = [U for ps_ in range(4) for U in units_of(ps_)]
                for ps_ in range(4):
                    us[8 * ps_]["ready"] = p0 + NCP * (ps_ + 1)
                return us

            def units_of(ps_):
                QB, KB, VB = QBs[ps_ % 2], KBs[ps_ % 2], VBs[ps_ % 2]
                out_ = []
                for hl in range(2):
                    for hp_ in range(2):
                        for t in range(2):
                            h = 4 * ps_ + 2 * hl + hp_
                            rows = slice(64 * hp_, 64 * hp_ + 64)
                            grp = 2 * ps_ + hl
                            tt = slice(t * P, (t + 1) * P)
                            if na:
                                sc = [(QB[rows, hl, tt], KB[rows, hl, :], 0, T)]
                                pv = [(VB[:, hl, j, rows], j * P) for j in range(2)]
                                nk = T
                                bias = NB[:, t, h, :]
                                soft = lambda S, ps, b=bias: nc.vector.scalar_tensor_tensor(
                                    S, ps, HD ** -0.5, b, ALU.mult, ALU.add)
                            else:
                                b = 3 * hl
                                sc = [(QB[rows, b, tt], KB[rows, b, :], 0, T),
                                      (QB[rows, b + 1, tt], KB[rows, b + 1, tt], T, P),
                                      (QB[rows, b + 2, tt], KB[rows, b + 2, tt], T + P, P)]
                                pv = [(VB[:, b, j, rows], j * P) for j in range(2)]
                                pv += [(VB[:, b + 1, t, rows], T), (VB[:, b + 2, t, rows], T + P)]
                                nk = 512
                                soft = lambda S, ps, t=t, h=h: nc.vector.scalar_tensor_tensor(
                                    S, DM[:, t, :], slopes[:, h:h + 1], ps, ALU.mult, ALU.add)
                            o = one_bank(grp)[rows, tt]
                            out_.append(dict(scores=sc, pv=pv, nk=nk, soft=soft, out=o, grp=grp,
                                             end=hp_ == 1 and t == 1))
                return out_

            def pe_f(pe, w):
                def tiles(c, j, bank, slot):
                    if j == 0:
                        tile_fm(bank, 0, slot)
                        return tile_fm(bank, 1, slot)
                    if j == 1:
                        tile_tm(bank, 0, slot)
                        return tile_fm(bank, 1, slot)
                    tile_fm(bank, 0, slot)
                    return tile_tm(bank, 1, slot)
                def proj(c, n):
                    proj_pe(pe, w, n, lambda c0, j, bank, slot: tiles(c0, (c + j) % 3, bank, slot))

                units = all_units(w.p)
                proj(0, NCP)
                pe.wait_ge(*at(tag, "tab", 1))
                attn_pe(pe, tag, units, 0, deep=1, after=lambda u: [proj(c, 1) for c in chunks_behind(u)])
                pe.wait_ge(*at(tag, "od", 8))
                out_pe(pe, w, 8, 8, tag, "od")

            def dve_f(dve, w):
                def evac(ps_, c):
                    dve.wait_ge(w_used, w.g + 1)
                    bank, (i, j) = pj[w.p % 3], divmod(c, 3)
                    QB, KB, VB = QBs[ps_ % 2], KBs[ps_ % 2], VBs[ps_ % 2]
                    qs = 1.0 if na else HD ** -0.5

                    def fm(half, d, scale):
                        return nc.vector.scalar_tensor_tensor(d, bank[:, half * T:(half + 1) * T], scale, rP[:, :],
                                                              ALU.mult, ALU.mult)

                    def tm(half, d):
                        for t in range(2):
                            x = nc.vector.tensor_scalar(d[:, t, :], bank[:, half * T + t * P:half * T + (t + 1) * P],
                                                        rsc[:, 2 + t:3 + t], None, ALU.mult)
                        return x
                    if j == 0:
                        fm(0, QB[:, 2 * i, :], qs)
                        x = fm(1, KB[:, 2 * i, :], 1.0)
                    elif j == 1:
                        tm(0, VB[:, 2 * i])
                        x = fm(1, QB[:, 2 * i + 1, :], qs)
                    else:
                        fm(0, KB[:, 2 * i + 1, :], 1.0)
                        x = tm(1, VB[:, 2 * i + 1])
                    x.then_inc(pj_free, 1)
                    w.g += 1
                    w.p += 1

                for c in range(NCP):
                    evac(0, c)
                dve.wait_ge(*at(tag, "tl", 16 * (17 if na else 1)))
                if na:
                    bias = NB.rearrange("p a h (r c) -> p (a h r) c", c=64)
                    link(dve, nc.vector.tensor_tensor(bias, bias, MK[:, None, :].to_broadcast([P, 2 * HEADS * 4, 64]),
                                                      ALU.add))
                nc.vector.tensor_copy(nt[:, 8:9], rsc[:, 2:3]).then_inc(sg(tag, "tab"), 1)

                def behind(u):
                    ps_ = u // 8
                    for c in chunks_behind(u):
                        if ps_ and c == 0:
                            dve.wait_ge(*at(tag, "pv", 8 * ps_))
                        evac(ps_ + 1, c)

                attn_dve(dve, tag, all_units(0), 0, lo_f(dve), after=behind,
                         busy=[u for u in range(32) if len(chunks_behind(u))])
                w.g += 4

            def act_f(act, w):
                act_phase(act, w, NCP, is_proj=True)
                attn_act(act, tag, all_units(0), 0, hi_f,
                         after=lambda u: [act_phase(act, w, 1, is_proj=True) for _ in chunks_behind(u)])
                out_act(act, w, 8)

            def load(sp):
                if na:
                    for i in range(4):
                        rows = slice(64 * (i % 2), 64 * (i % 2) + 64)
                        for r in range(4):
                            src = bass.AP(tensor=rpb.tensor, offset=(7 - i + r) * 31 + 15,
                                          ap=[[HEADS * 465, 64], [465, HEADS], [1, 64]])
                            sp.dma_start(NB[rows, i // 2, :, r * 64:(r + 1) * 64], src).then_inc(sg(tag, "tl"), 16)
                    sp.dma_start(MK, c_dram("na_mask")).then_inc(sg(tag, "tl"), 16)
                else:
                    sp.dma_start(DM.rearrange("p a n -> p (a n)"), c_dram("dist")).then_inc(sg(tag, "tl"), 16)
            return pe_f, dve_f, act_f, load

        def xattn(tag, kind):
            XH = 4
            take = arena()
            take(16, T)
            MR = take(KT, T)
            MS = take(KT, T)
            Q = take(XH, T)
            Kb = take(XH, T)
            V = take(2, XH * P)
            rM = take(T)
            hi_f, lo_f = split_out(tag, False)
            rs = nt[:, 12:14]
            mt = tag + "m"

            units = [dict(scores=[(Q[:, h, t * P:(t + 1) * P], Kb[:, h, :], 0, T)],
                          pv=[(V[:, j, h * P:(h + 1) * P], j * P) for j in range(2)], nk=T,
                          soft=lambda S, ps: nc.vector.tensor_scalar(S, ps, P ** -0.5, None, ALU.mult),
                          out=o_bank(h)[:, t * P:(t + 1) * P], grp=h, end=t == 1)
                     for h in range(XH) for t in range(2)]

            def pe_f(pe, w):
                def q_tiles(c, j, bank, slot):
                    tile_fm(bank, 0, slot)
                    return tile_fm(bank, 1, slot)

                def k_tiles(c, j, bank, slot):
                    tile_fm(bank, 0, slot, AR, AR, 16, 24)
                    return tile_fm(bank, 1, slot, AR, AR, 16, 24)

                def v_tiles(c, j, bank, slot):
                    tile_tm(bank, 0, slot, AR, AR, off=16, lofs=24)
                    return tile_tm(bank, 1, slot, AR, AR, off=16, lofs=24)
                proj_pe(pe, w, 2, q_tiles)
                pe.wait_ge(*at(tag + "pre", "rb", 1))
                stats_pe(pe, mt, MS)
                bcast_pe(pe, mt, rs)
                pe.wait_ge(*at(mt, "lo", KT))
                proj_pe(pe, w, 2, k_tiles)
                proj_pe(pe, w, 2, v_tiles)
                pe.wait_ge(pj_free, 3 + w.p)
                attn_pe(pe, tag, units, 0)
                out_pe(pe, w, 4, 8, tag, "od")

            def dve_f(dve, w):
                def fm(dst, scaled):
                    def body(c, g, gs, it, p, ps):
                        dve.wait_ge(w_used, g + 1)
                        src = pj[ps][:, :].rearrange("p (a t) -> p a t", a=2)
                        d = dst[:, 2 * c:2 * c + 2, :]
                        if scaled:
                            x = nc.vector.tensor_tensor(d, src, rP[:, None, :].to_broadcast([P, 2, T]), ALU.mult)
                        else:
                            x = nc.vector.tensor_copy(d, src)
                        x.then_inc(pj_free, 1)
                    chunk_loop(dve, w, 2, body, is_proj=True)
                fm(Q, True)
                stats_dve(dve, mt, rs, 1.0 / D, EPS)
                bcast_dve(dve, mt, rM)
                for k in range(KT):
                    nc.vector.scalar_tensor_tensor(MR[:, k, :], MR[:, k, :], v("mem_g", k), rM, ALU.mult, ALU.mult)\
                        .then_inc(sg(mt, "n"), 1)
                for k in range(KT):
                    dve.wait_ge(*at(mt, "hi", k + 1))
                    nc.vector.tensor_tensor(AR[:, 24 + k, :], MR[:, k, :], AR[:, 16 + k, :].bitcast(F32),
                                            ALU.subtract).then_inc(sg(mt, "lo"), 1)
                fm(Kb, False)

                def vbody(c, g, gs, it, p, ps):
                    dve.wait_ge(w_used, g + 1)
                    nc.vector.tensor_copy(V[:, :, 2 * c * P:(2 * c + 2) * P].rearrange("p t (a n) -> p a t n", a=2),
                                          pj[ps][:, :].rearrange("p (a t n) -> p a t n", a=2, t=2))\
                        .then_inc(pj_free, 1)
                chunk_loop(dve, w, 2, vbody, is_proj=True)
                attn_dve(dve, tag, units, 0, lo_f(dve))
                w.g += 2

            def act_f(act, w):
                act.wait_ge(*at(mt, "ld", 16))
                for k in range(KT):
                    nc.scalar.activation(MS[:, k, :], MR[:, k, :], ACT.Square).then_inc(sg(mt, "sq"), 1)
                act_phase(act, w, 2, is_proj=True)
                for k in range(KT):
                    act.wait_ge(*at(mt, "n", k + 1))
                    nc.scalar.activation(AR[:, 16 + k, :], MR[:, k, :], ACT.Copy).then_inc(sg(mt, "hi"), 1)
                act_phase(act, w, 4, is_proj=True)
                attn_act(act, tag, units, 0, hi_f)
                out_act(act, w, 4)

            def load(act):
                act.dma_start(MR, memin).then_inc(sg(mt, "ld"), 16)
            return pe_f, dve_f, act_f, load

        def dsa(tag, kind):
            DH, TOPK = 8, 64
            take = arena()
            CQ = take(3, T)
            C2 = take(3, T)
            CK = take(T)
            WI = take(2, 8)
            HB = take(12, T)
            U = take(4, T + 2)
            SM = take(3072)
            UQ, QIw, UK, UV = SM[:, 0:1024], SM[:, 1024:2048], SM[:, 2048:2560], SM[:, 2560:3072]
            QT = take(4, T)
            QI = take(4, T)
            CT = take(2, P)
            QL = take(8, T)
            OL = take(8, T)
            RL = take(2, 2, T)
            SC = take(2, T)
            MBs = take(2, T)
            CA = take(2, T)
            M8 = take(2, 8)
            hb, bb, cb_ = HB[:, 0:4, :], HB[:, 4:8, :], HB[:, 8:12, :]
            dst_tiles = [CQ[:, 0], CQ[:, 1], CQ[:, 2], CK, None] + [HB[:, i] for i in range(12)] + [None]
            S = lambda n: sem(f"{tag}_{n}")
            M = Sb[:, 0, 0:T]

            def ql(h):
                return 4 * (h % 2) + h // 2

            units = []
            for h in range(DH):
                for t in range(2):
                    units.append(dict(
                        scores=[(QL[:, ql(h), t * P:(t + 1) * P], CQ[:, 2, :], 0, T)],
                        pv=[(CT[:, j, :], j * P) for j in range(2)], nk=T,
                        soft=lambda s_, ps, t=t: nc.vector.scalar_tensor_tensor(s_, ps, 64 ** -0.5, MBs[:, t, :],
                                                                               ALU.mult, ALU.add),
                        out=o_bank(h)[:, t * P:(t + 1) * P], grp=h, end=t == 1))

            def lbank(v_, odd):
                return ([pj[2], mb] if odd else [pj[0], pj[1]])[v_ % 2][:, 0:T]

            def pe_f(pe, w):
                def tiles(c, j, bank, slot):
                    for half in range(2):
                        i = 2 * c + half
                        if i == 4:
                            last = tile_tm(bank, half, slot, n=8)
                        elif i < 17:
                            last = tile_fm(bank, half, slot)
                    return last
                for c in range(9):
                    proj_pe(pe, w, 1, lambda c0, j, bank, slot, c=c: tiles(c, j, bank, slot))
                pe.wait_ge(S("sq"), 3)
                for t in range(2):
                    for k in range(2):
                        nc.tensor.matmul(mb[:, 508 + t:509 + t], C2[:, k, t * P:(t + 1) * P], ones[:, 0:1],
                                         start=k == 0, stop=k == 1)
                for t in range(2):
                    last = nc.tensor.matmul(mb[:, 510 + t:511 + t], C2[:, 2, t * P:(t + 1) * P], ones[:, 0:1],
                                            start=True, stop=True)
                last.then_inc(S("st"), 1)
                pe.wait_ge(S("rs"), 1)
                for i in range(4):
                    last = nc.tensor.matmul(acc[0][:, i * P:(i + 1) * P], nt[:, 8 + i:9 + i].to_broadcast([P, P]),
                                            ident, start=True, stop=True)
                last.then_inc(S("bc"), 1)
                pe.wait_ge(S("cn"), 3)
                pe.wait_ge(S("ld"), 32)
                for W, banks in ((UQ, (acc[1], acc[2])), (QIw, (acc[3], pj[0]))):
                    for i in range(4):
                        for k in range(2):
                            last = nc.tensor.matmul(banks[i // 2][:, (i % 2) * T:(i % 2 + 1) * T],
                                                    W[:, k * 512 + i * P:k * 512 + (i + 1) * P], CQ[:, k, :],
                                                    start=k == 0, stop=k == 1)
                    last.then_inc(S("q"), 1)
                for j in range(2):
                    last = nc.tensor.transpose(mb[:, j * P:(j + 1) * P], CQ[:, 2, j * P:(j + 1) * P], ident)
                last.then_inc(S("q"), 1)
                pe.wait_ge(S("qc"), 5)
                for h in (0, 2, 4, 6, 1, 3, 5, 7):
                    rows = slice(64 * (h % 2), 64 * (h % 2) + 64)
                    bank = acc[2 * (h % 2) + h // 4]
                    last = nc.tensor.matmul(bank[:, (h // 2 % 2) * T:(h // 2 % 2 + 1) * T],
                                            UK[rows, (h // 2) * P:(h // 2 + 1) * P], QT[rows, h // 2, :],
                                            start=True, stop=True)
                last.then_inc(S("ql"), 1)
                for v_ in range(8):
                    t, a = divmod(v_, 4)
                    if v_ >= 2:
                        pe.wait_ge(S("relu"), v_ - 1)
                    for odd in range(2):
                        rows = slice(64 * odd, 64 * odd + 64)
                        last = nc.tensor.matmul(lbank(v_, odd), QI[rows, a, t * P:(t + 1) * P], CK[rows, :],
                                                start=True, stop=True)
                    last.then_inc(S("lg"), 1)
                pe.wait_ge(S("qlc"), 4)
                pe.wait_ge(S("mask"), 1)
                attn_pe(pe, tag, units, 0)
                pe.wait_ge(*at(tag, "od", DH))
                for h in range(DH):
                    rows = slice(64 * (h % 2), 64 * (h % 2) + 64)
                    last = nc.tensor.matmul(acc[h // 4][rows, (h // 2 % 2) * T:(h // 2 % 2 + 1) * T],
                                            UV[:, h * 64:(h + 1) * 64], OL[:, h, :], start=True, stop=True)
                last.then_inc(S("o"), 1)
                pe.wait_ge(S("rdy"), 8)
                out_pe(pe, w, 8, 8, tag, "rdy")

            def dve_f(dve, w):
                for c in range(9):
                    dve.wait_ge(w_used, w.g + 1)
                    bank = pj[w.p % 3]
                    for half in range(2):
                        i = 2 * c + half
                        src = bank[:, half * T:(half + 1) * T]
                        if i == 4:
                            for t in range(2):
                                x = nc.vector.tensor_scalar(WI[:, t, :], src[:, t * P:t * P + 8], rsc[:, 2 + t:3 + t],
                                                            512 ** -0.5, ALU.mult, ALU.mult)
                        elif i < 17:
                            x = nc.vector.tensor_tensor(dst_tiles[i], src, rP[:, :], ALU.mult)
                    x.then_inc(pj_free, 1)
                    w.g += 1
                    w.p += 1
                dve.wait_ge(S("st"), 1)
                link(dve, nc.vector.tensor_scalar(nt[:, 0:2], mb[:, 508:510], 1.0 / 256, EPS, ALU.mult, ALU.add))
                link(dve, nc.vector.tensor_scalar(nt[:, 2:4], mb[:, 510:512], 1.0 / 128, EPS, ALU.mult, ALU.add))
                rsqrt(dve, nt[:, 8:12], nt[:, 0:4], 4, nt[:, 4:8], nt[:, 12:16])
                nc.vector.tensor_copy(nt[:, 0:4], nt[:, 8:12]).then_inc(S("rs"), 1)
                dve.wait_ge(S("bc"), 1)
                for k in range(3):
                    nc.vector.scalar_tensor_tensor(CQ[:, k, :], CQ[:, k, :], v("qn", k) if k < 2 else v("kvn", 0),
                                                   acc[0][:, (k // 2) * T:(k // 2 + 1) * T], ALU.mult, ALU.mult)\
                        .then_inc(S("cn"), 1)
                nc.vector.memset(U[:, :, 0:2], 0.0)
                link(dve, nc.vector.tensor_tensor(U[:, :, 2:T + 2], cb_, hb, ALU.mult))
                dve.wait_ge(S("cn"), 3)
                for k in range(4):
                    y = hb[:, k, :]
                    link(dve, nc.vector.tensor_scalar(y, U[:, k, 0:T], v("cw0", k), v("cb", k), ALU.mult, ALU.add))
                    link(dve, nc.vector.scalar_tensor_tensor(y, U[:, k, 1:T + 1], v("cw1", k), y, ALU.mult, ALU.add))
                    link(dve, nc.vector.scalar_tensor_tensor(y, U[:, k, 2:T + 2], v("cw2", k), y, ALU.mult, ALU.add))
                    nc.vector.tensor_tensor(y, y, bb[:, k, :], ALU.mult).then_inc(S("cv"), 1)
                for v_ in range(8):
                    t, a = divmod(v_, 4)
                    dve.wait_ge(S("relu"), v_ + 1)
                    for odd in range(2):
                        h = 2 * a + odd
                        if h == 0:
                            x = nc.vector.tensor_scalar(SC[:, t, :], RL[:, 0, 0, :] if v_ % 2 == 0 else RL[:, 1, 0, :],
                                                        WI[:, t, 0:1], None, ALU.mult)
                        else:
                            x = nc.vector.scalar_tensor_tensor(SC[:, t, :], RL[:, v_ % 2, odd, :], WI[:, t, h:h + 1],
                                                               SC[:, t, :], ALU.mult, ALU.add)
                        if odd == 0:
                            link(dve, x)
                    x.then_inc(S("sc"), 1)
                    dve.wait_ge(S("sc"), v_ + 1)
                dve.wait_ge(S("ld"), 32)
                link(dve, nc.vector.tensor_tensor(SC, SC, CA, ALU.add))
                for _ in range(TOPK // 8):
                    for t in range(2):
                        link(dve, nc.vector.max(M8[:, t, :], SC[:, t, :]))
                    for t in range(2):
                        link(dve, nc.vector.match_replace(SC[:, t, :], M8[:, t, :], SC[:, t, :], -3e38))
                link(dve, nc.vector.tensor_scalar(MBs, SC, -2e38, 1e30, ALU.is_lt, ALU.mult))
                nc.vector.scalar_tensor_tensor(MBs, MBs, -1e30, CA, ALU.add, ALU.add).then_inc(S("mask"), 1)
                dve.wait_ge(S("mask"), 1)
                attn_dve(dve, tag, units, 0, lambda grp: None)
                for k in range(8):
                    kt = (k + 4) % 8
                    dve.wait_ge(S("oh"), k + 1 if k < 4 else 8)
                    src = hb[:, kt - 4, :] if kt >= 4 else acc[kt // 2][:, (kt % 2) * T:(kt % 2 + 1) * T]
                    nc.vector.tensor_tensor(AR[:, 8 + kt, :], src, AR[:, kt, :].bitcast(F32), ALU.subtract)\
                        .then_inc(S("rdy"), 1)
                w.g += 4

            def act_f(act, w):
                for c in range(9):
                    act_phase(act, w, 1, is_proj=True)
                    if c == 1:
                        act.wait_ge(pj_free, 3 + w.p)
                        for k in range(3):
                            nc.scalar.activation(C2[:, k, :], CQ[:, k, :], ACT.Square).then_inc(S("sq"), 1)
                act.wait_ge(S("q"), 3)
                for d, bank in ((QT[:, 0:2], acc[1]), (QT[:, 2:4], acc[2]), (QI[:, 0:2], acc[3]), (QI[:, 2:4], pj[0])):
                    nc.scalar.activation(d.rearrange("p a t -> p (a t)"), bank[:, :], ACT.Copy).then_inc(S("qc"), 1)
                nc.scalar.activation(CT.rearrange("p a t -> p (a t)"), mb[:, 0:T], ACT.Copy).then_inc(S("qc"), 1)
                act.wait_ge(S("ql"), 1)
                for b in range(4):
                    nc.scalar.activation(QL[:, 2 * b:2 * b + 2, :].rearrange("p a t -> p (a t)"), acc[b][:, :],
                                         ACT.Copy).then_inc(S("qlc"), 1)
                for v_ in range(8):
                    act.wait_ge(S("lg"), v_ + 1)
                    if v_ >= 2:
                        act.wait_ge(S("sc"), v_ - 1)
                    for odd in range(2):
                        x = nc.scalar.activation(RL[:, v_ % 2, odd, :], lbank(v_, odd), ACT.Relu)
                    x.then_inc(S("relu"), 1)

                def fin(grp):
                    nc.scalar.activation(OL[:, grp, :], o_bank(grp), ACT.Copy).then_inc(sg(tag, "od"), 1)
                attn_act(act, tag, units, 0, fin)
                act.wait_ge(S("cv"), 4)
                for k in range(4):
                    nc.scalar.activation(AR[:, 4 + k, :], hb[:, k, :], ACT.Copy).then_inc(S("oh"), 1)
                act.wait_ge(S("o"), 1)
                for k in range(4):
                    nc.scalar.activation(AR[:, k, :], acc[k // 2][:, (k % 2) * T:(k % 2 + 1) * T], ACT.Copy)\
                        .then_inc(S("oh"), 1)
                out_act(act, w, 8)

            def load(act):
                a, n = SCOL["uq"]
                act.dma_start(SM, small[:, a:a + 3072]).then_inc(S("ld"), 16)
                act.dma_start(CA.rearrange("p a t -> p (a t)"), c_dram("causal")).then_inc(S("ld"), 16)
            return pe_f, dve_f, act_f, load

        def group_norm(dve, Y, n, sq, st, eps):
            m = Y.shape[1]
            link(dve, nc.vector.tensor_reduce(st[:, 0:m], Y, AXX, ALU.add))
            link(dve, nc.vector.tensor_scalar(st[:, 0:m], st[:, 0:m], 1.0 / n, None, ALU.mult))
            link(dve, nc.vector.tensor_tensor(Y, Y, st[:, 0:m].unsqueeze(2).to_broadcast([P, m, n]), ALU.subtract))
            link(dve, nc.vector.tensor_tensor(sq, Y, Y, ALU.mult))
            link(dve, nc.vector.tensor_reduce(st[:, m:2 * m], sq, AXX, ALU.add))
            link(dve, nc.vector.tensor_scalar(st[:, m:2 * m], st[:, m:2 * m], 1.0 / n, eps, ALU.mult, ALU.add))
            rsqrt(dve, st[:, 0:m], st[:, m:2 * m], m, st[:, 2 * m:3 * m], st[:, 3 * m:4 * m])
            return nc.vector.tensor_tensor(Y, Y, st[:, 0:m].unsqueeze(2).to_broadcast([P, m, n]), ALU.mult)

        def rwrt(tag, kind):
            RH, C = 8, 64
            assert FS >= 21000

            def f(at, *shape):
                n = int(np.prod(shape))
                a = F0[:, at:at + n]
                if len(shape) == 2:
                    a = a.rearrange("p (a b) -> p a b", b=shape[1])
                elif len(shape) == 3:
                    a = a.rearrange("p (a b c) -> p a b c", b=shape[1], c=shape[2])
                elif len(shape) == 4:
                    a = a.rearrange("p (a b c d) -> p a b c d", b=shape[1], c=shape[2], d=shape[3])
                return a
            ART = f(0, 4, 2, 2, P)
            BT = f(2048, 4, T)
            KTt = f(3072, 4, T)
            Z = f(2048, 16, P)
            V = f(4096, 4, T)
            G = f(5120, 4, T)
            TM = f(6144, 3, 2, 512)
            XWG = f(6144, 2, T)
            SCANM = f(6656, T)
            WA2 = f(6912, 512)
            G2 = f(7424, 512)
            AMASK = f(9216, 512)
            LEV = f(9728, 6, P)
            EC = f(10496, 4, 4)
            W1 = f(10560, 2, 512)
            YP = f(11584, 2, 512)
            AM = f(12608, 16, 4, P)
            R, K_, LD, A, KK, L, E1, E2 = (f(12608 + 1024 * i, 4, T) for i in range(8))
            T1, T2 = f(10560, 4, T), f(11584, 4, T)
            SS = Sb[:, :, :].rearrange("p a n -> p (a n)")
            KS = PTb[:, :, :].rearrange("p (b a) (c n) -> p (b a c) n", b=1, n=T)
            ZT = [Sb[:, a, :].rearrange("p (u n) -> p u n", n=P) for a in range(2)] + \
                 [PTb[:, a, :].rearrange("p (u n) -> p u n", n=P) for a in range(2)]
            ST = Sb[:, :, :].rearrange("p a (b h n) -> p (a b) h n", b=2, n=C)
            X1 = PTb[:, 0, :]
            TP = [Sb[:, 0, 0:T + 1], Sb[:, 1, 0:T + 1]]
            SH = PTb[:, 0, 0:T]
            q0 = 14656
            RQ, RK = f(0, 4, T), f(1024, 4, T)
            RV = f(2048, 2, 512)
            RG = f(3072, 4, T)
            DEC = f(7936, 4, 512)
            ROC, ROS = f(9984, T), f(10240, T)
            STt = f(q0, 4, 2, T)
            O = f(q0 + 2048, 2, 512)
            O2 = f(q0 + 3072, 2, 512)
            TG = f(q0 + 4096, 4, T)
            HW0, HA0 = nt[:, 8:12], nt[:, 12:16]
            SWP = f(10560, P)
            rt_stat = f(10700, 64)
            M2 = f(5120, T)
            YF = f(0, 4, T)
            rw_stat = AM[:, 8, 3, :]
            Sx = lambda n: sem(f"{tag}_{n}")
            RKs = P ** -0.5
            LAM = float(np.exp(-0.5))

            def hrows(h):
                return slice(64 * (h % 2), 64 * (h % 2) + 64)

            def u4(bank):
                return bank[:, :].rearrange("p (a n) -> p a n", n=P)

            def pe_f(pe, w):
                tt = lambda t: slice(t * P, (t + 1) * P)
                for c in range(15):
                    def tiles(c0, j, bank, slot, c=c):
                        if c in (4, 5):
                            tile_tm(bank, 0, slot)
                            return tile_tm(bank, 1, slot)
                        tile_fm(bank, 0, slot)
                        return tile_fm(bank, 1, slot)
                    proj_pe(pe, w, 1, tiles)
                pe.wait_ge(pj_free, 3 + w.p)
                pe.wait_ge(Sx("ld"), 16 * 7)
                for i in range(8):
                    last = nc.tensor.matmul(acc[i // 2][:, (i % 2) * T:(i % 2 + 1) * T], SWP,
                                            (RQ if i < 4 else RK)[:, i % 4, :], start=True, stop=True)
                last.then_inc(Sx("sw"), 1)
                rb = [pj[0], pj[1], pj[2], mb]
                for h in range(4):
                    pe.wait_ge(Sx("rot"), 5 + h)
                    for st in range(2):
                        last = nc.tensor.matmul(rb[h][:, st * T:(st + 1) * T], RK[:, h, tt(st)], RQ[:, h, :],
                                                start=True, stop=True)
                    last.then_inc(Sx("rs"), 1)
                for h in range(4):
                    pe.wait_ge(Sx("rd"), h + 1)
                    for t in range(2):
                        for st in range(t + 1):
                            last = nc.tensor.matmul(acc[t][:, h * P:(h + 1) * P], STt[:, h, st, tt(t)],
                                                    RV[:, st, h * P:(h + 1) * P], start=st == 0, stop=st == t)
                last.then_inc(Sx("ro"), 1)
                pe.wait_ge(Sx("gn"), 1)
                for h in range(4):
                    for t in range(2):
                        last = nc.tensor.transpose(acc[2 + h // 2][:, (h % 2) * T + t * P:(h % 2) * T + (t + 1) * P],
                                                   O[:, t, h * P:(h + 1) * P], ident)
                last.then_inc(Sx("rt"), 1)
                pe.wait_ge(Sx("lin"), 3)
                pe.wait_ge(Sx("rend"), 4)
                for i in range(4):
                    nc.tensor.matmul(pj[i // 2][:, (i % 2) * T:(i % 2 + 1) * T], WA2[0:64, i * P:(i + 1) * P],
                                     XWG[0:64, 0, :], start=True, stop=True)
                for i in range(4):
                    nc.tensor.matmul(acc[i // 2][:, (i % 2) * T:(i % 2 + 1) * T], WA2[64:128, i * P:(i + 1) * P],
                                     XWG[64:128, 0, :], start=True, stop=True)
                for i in range(4):
                    last = nc.tensor.matmul(acc[2 + i // 2][:, (i % 2) * T:(i % 2 + 1) * T], G2[:, i * P:(i + 1) * P],
                                            XWG[:, 1, :], start=True, stop=True)
                last.then_inc(Sx("lr"), 1)
                pe.wait_ge(Sx("kks"), 1)
                for i in range(4):
                    last = nc.tensor.matmul((pj[2], mb)[i // 2][:, (i % 2) * T:(i % 2 + 1) * T], blk, KS[:, i, :],
                                            start=True, stop=True)
                last.then_inc(Sx("ss"), 1)
                for t in range(2):
                    if t == 0:
                        pe.wait_ge(Sx("lrd"), 6)
                    for i in range(4):
                        last = nc.tensor.transpose(acc[t][:, i * P:(i + 1) * P], V[:, i, tt(t)], ident)
                    last.then_inc(Sx("vt"), 1)
                pe.wait_ge(Sx("bon"), 1)
                for i in range(4):
                    last = nc.tensor.matmul(acc[2 + i // 2][:, (i % 2) * T:(i % 2 + 1) * T], blk, T1[:, i, :],
                                            start=True, stop=True)
                last.then_inc(Sx("bs"), 1)
                pe.wait_ge(Sx("tld"), 4)
                pe.wait_ge(Sx("vtc"), 2)
                for x, src in enumerate((BT, KTt)):
                    for t in range(2):
                        bank = (acc[0], acc[1], pj[0], pj[1])[2 * x + t]
                        for i in range(4):
                            last = nc.tensor.transpose(bank[:, i * P:(i + 1) * P], src[:, i, tt(t)], ident)
                        last.then_inc(Sx("tt"), 1)
                pe.wait_ge(Sx("bvd"), 1)
                ub = [acc[2], acc[3], pj[2], mb]
                for u in range(16):
                    t, h = divmod(u, 8)
                    rr = hrows(h)
                    if u >= 4:
                        pe.wait_ge(Sx("am"), u - 3)
                    ar = ART[rr, h // 2, t, :, :].rearrange("p a n -> p (a n)")
                    nc.tensor.matmul(ub[u % 4][:, 0:T], BT[rr, h // 2, tt(t)], ar, start=True, stop=True)
                    last = nc.tensor.matmul(ub[u % 4][:, T:2 * T], KTt[rr, h // 2, tt(t)], ar, start=True, stop=True)
                    last.then_inc(Sx("ap"), 1)
                pe.wait_ge(Sx("am"), 16)
                pe.wait_ge(Sx("ttc"), 4)
                for kind_, banks in ((2, (acc[0], acc[1])), (3, (pj[0], pj[1]))):
                    for u in range(16):
                        t, h = divmod(u, 8)
                        last = nc.tensor.matmul(banks[t][:, h * C:(h + 1) * C], AM[:, u, kind_, :],
                                                TM[:, 2, t, h * C:(h + 1) * C], start=True, stop=True)
                    last.then_inc(Sx("wy"), 1)
                zb = [acc[2], acc[3], pj[2], mb]
                for lv in range(6):
                    for g in range(4):
                        pe.wait_ge(Sx("E"), 4 * lv + g + 1)
                        pe.wait_ge(Sx("zt"), 4 * lv + g + 1)
                        if lv:
                            pe.wait_ge(Sx("zn"), 4 * (lv - 1) + g + 1)
                        for j in range(4):
                            u = 4 * g + j
                            last = nc.tensor.matmul(zb[g][:, j * P:(j + 1) * P], AM[:, u, 2, :], ZT[g][:, j, :],
                                                    start=True, stop=True)
                        last.then_inc(Sx("Qp"), 1)
                    for g in range(4):
                        pe.wait_ge(Sx("Q"), 4 * lv + g + 1)
                        if lv == 0 and g == 0:
                            pe.wait_ge(Sx("wyc"), 4)
                        za = (acc[0], acc[1], pj[0], pj[1])[g]
                        for j in range(4):
                            u = 4 * g + j
                            last = nc.tensor.matmul(za[:, j * P:(j + 1) * P], AM[:, u, 3, :], Z[:, u, :],
                                                    start=True, stop=True)
                        last.then_inc(Sx("Zp"), 1)
                        if lv < 5:
                            for j in range(4):
                                u = 4 * g + j
                                last = nc.tensor.matmul(zb[g][:, j * P:(j + 1) * P], Z[:, u, :], AM[:, u, 3, :],
                                                        start=True, stop=True)
                            last.then_inc(Sx("ZTp"), 1)
                pe.wait_ge(Sx("zn"), 24)
                yb = [pj[0], pj[1], pj[2], mb]
                for c in range(4):
                    t, half = divmod(c, 2)
                    cr = slice(64 * half, 64 * half + 64)
                    if c:
                        pe.wait_ge(Sx("S"), c)
                        for h in range(RH):
                            nc.tensor.matmul(acc[h % 2][cr, (h // 2) * C:(h // 2 + 1) * C],
                                             ART[hrows(h), h // 2, t, 0, cr], ST[hrows(h), c - 1, h // 2, :],
                                             start=True, stop=True)
                        for h in range(RH):
                            last = nc.tensor.matmul(yb[2 * t + h % 2][cr, (h // 2) * C:(h // 2 + 1) * C],
                                                    ART[hrows(h), h // 2, t, 1, cr], ST[hrows(h), c - 1, h // 2, :],
                                                    start=True, stop=True)
                        last.then_inc(Sx("x"), 1)
                        pe.wait_ge(Sx("X"), c)
                    for h in range(RH):
                        last = nc.tensor.matmul(acc[2][cr, h * C:(h + 1) * C], Z[cr, 8 * t + h, cr],
                                                X1[cr, h * C:(h + 1) * C] if c else W1[cr, 0, h * C:(h + 1) * C],
                                                start=True, stop=True)
                    last.then_inc(Sx("up"), 1)
                    pe.wait_ge(Sx("U"), c + 1)
                    if c < 3:
                        for h in range(RH):
                            o = acc[3][hrows(h), (h // 2) * C:(h // 2 + 1) * C]
                            nc.tensor.matmul(o, TM[cr, 0, t, h * C:(h + 1) * C],
                                             AM[cr, 4 * t + h // 2, 2, (h % 2) * C:(h % 2 + 1) * C],
                                             start=True, stop=False)
                            last = nc.tensor.matmul(o, TM[cr, 1, t, h * C:(h + 1) * C],
                                                    TM[cr, 2, t, h * C:(h + 1) * C], start=False, stop=True)
                        last.then_inc(Sx("sp"), 1)
                for t in range(2):
                    for h in range(RH):
                        last = nc.tensor.matmul(acc[t][:, h * C:(h + 1) * C], AM[:, 8 * t + h, 1, :],
                                                AM[:, 4 * t + h // 2, 2, (h % 2) * C:(h % 2 + 1) * C],
                                                start=True, stop=True)
                last.then_inc(Sx("y2"), 1)
                pe.wait_ge(Sx("ygn"), 1)
                for i in range(4):
                    for t in range(2):
                        last = nc.tensor.transpose(acc[2 + i // 2][:, (i % 2) * T + t * P:(i % 2) * T + (t + 1) * P],
                                                   YP[:, t, i * P:(i + 1) * P], ident)
                last.then_inc(Sx("yt"), 1)
                pe.wait_ge(Sx("rdy"), 8)
                out_pe(pe, w, 8, 8, tag, "rdy")

            def dve_f(dve, w):
                nc.vector.memset(Sb[:, 0, 0:1], 0.0)
                nc.vector.memset(Sb[:, 1, 0:1], 0.0).then_inc(Sx("pad"), 1)
                dve.wait_ge(Sx("pad"), 1)
                rw_dst = [R[:, i] for i in range(4)] + [K_[:, i] for i in range(4)] + [V[:, i] for i in range(4)] \
                    + [XWG[:, 0], XWG[:, 1]]
                for c in range(15):
                    dve.wait_ge(w_used, w.g + 1)
                    bank = pj[w.p % 3]
                    for half in range(2):
                        src = bank[:, half * T:(half + 1) * T]
                        i = 2 * c + half
                        if i < 4:
                            x = nc.vector.tensor_tensor(RQ[:, i, :], src, rP[:, :], ALU.mult)
                        elif i < 8:
                            x = nc.vector.scalar_tensor_tensor(RK[:, i - 4, :], src, RKs, rP[:, :], ALU.mult, ALU.mult)
                        elif i < 12:
                            for t in range(2):
                                x = nc.vector.tensor_scalar(RV[:, t, (i - 8) * P:(i - 7) * P], src[:, t * P:(t + 1) * P],
                                                            rsc[:, 2 + t:3 + t], None, ALU.mult)
                        elif i < 16:
                            x = nc.vector.tensor_tensor(RG[:, i - 12, :], src, rP[:, :], ALU.mult)
                        else:
                            n = i - 16
                            tp = TP[n % 2]
                            link(dve, nc.vector.tensor_tensor(tp[:, 1:T + 1], src, rP[:, :], ALU.mult))
                            link(dve, nc.vector.tensor_tensor(SH, tp[:, 0:T], tp[:, 1:T + 1], ALU.subtract))
                            x = nc.vector.scalar_tensor_tensor(rw_dst[n], SH, v("mu", n), tp[:, 1:T + 1],
                                                               ALU.mult, ALU.add)
                    x.then_inc(pj_free, 1)
                    w.g += 1
                    w.p += 1
                dve.wait_ge(pj_free, 3 + w.p)
                dve.wait_ge(Sx("ld"), 16 * 7)
                dve.wait_ge(Sx("sw"), 1)
                for n, i in enumerate((4, 5, 6, 7, 0, 1, 2, 3)):
                    if n:
                        dve.wait_ge(Sx("rot"), n)
                    X = (RQ if i < 4 else RK)[:, i % 4, :]
                    link(dve, nc.vector.tensor_tensor(M2, acc[i // 2][:, (i % 2) * T:(i % 2 + 1) * T], ROS, ALU.mult))
                    link(dve, nc.vector.tensor_tensor(X, X, ROC, ALU.mult))
                    nc.vector.tensor_tensor(X, X, M2, ALU.add).then_inc(Sx("rot"), 1)
                rb = [pj[0], pj[1], pj[2], mb]
                for h in range(4):
                    dve.wait_ge(Sx("rs"), h + 1)
                    nc.vector.tensor_tensor(STt[:, h].rearrange("p a t -> p (a t)"), rb[h][:, :], DEC[:, h, :],
                                            ALU.mult).then_inc(Sx("rd"), 1)
                dve.wait_ge(Sx("ro"), 1)
                for t in range(2):
                    link(dve, nc.vector.tensor_copy(O[:, t, :], acc[t][:, :]))
                group_norm(dve, O.rearrange("p t (h n) -> p (t h) n", n=P), P,
                           O2.rearrange("p t (h n) -> p (t h) n", n=P), rt_stat, EPS).then_inc(Sx("gn"), 1)
                dve.wait_ge(Sx("rt"), 1)
                dve.wait_ge(Sx("tg"), 1)
                for h in range(4):
                    Y = O2[:, h // 2, (h % 2) * T:(h % 2 + 1) * T]
                    link(dve, nc.vector.tensor_scalar(Y, acc[2 + h // 2][:, (h % 2) * T:(h % 2 + 1) * T], v("gn_g", h),
                                                      v("gn_b", h), ALU.mult, ALU.add))
                    link(dve, nc.vector.scalar_tensor_tensor(TG[:, h, :], TG[:, h, :], 1.0, RG[:, h, :],
                                                             ALU.add, ALU.mult))
                    nc.vector.scalar_tensor_tensor(Y, TG[:, h, :], 0.5, Y, ALU.mult, ALU.mult)\
                        .then_inc(Sx("rend"), 1)
                for h in range(4):
                    dve.wait_ge(Sx("rhi"), h + 1)
                    Y = O2[:, h // 2, (h % 2) * T:(h % 2 + 1) * T]
                    nc.vector.tensor_tensor(AR[:, 12 + h, :], Y, AR[:, 4 + h, :].bitcast(F32), ALU.subtract)\
                        .then_inc(Sx("rdy"), 1)
                dve.wait_ge(Sx("rdy"), 4)
                for i in range(4):
                    nc.vector.tensor_scalar(KK[:, i, :], K_[:, i, :], v("k_k", i), None, ALU.mult)\
                        .then_inc(Sx("kk"), 1)
                nc.vector.tensor_scalar(HW0, vecs[:, VCOL["w0"]:VCOL["w0"] + 4], 0.5, None, ALU.mult)
                nc.vector.tensor_scalar(HA0, vecs[:, VCOL["a0"]:VCOL["a0"] + 4], 0.5, None, ALU.mult)\
                    .then_inc(Sx("h0"), 1)
                dve.wait_ge(Sx("sxg"), 1)
                nc.vector.tensor_scalar(XWG[:, 1, :], XWG[:, 1, :], 0.5, 0.5, ALU.mult, ALU.add)\
                    .then_inc(Sx("lin"), 1)
                dve.wait_ge(Sx("ss"), 1)
                for b in range(2):
                    link(dve, nc.vector.tensor_scalar(SS[:, b * 512:(b + 1) * 512], (pj[2], mb)[b][:, :], 1e-24, None,
                                                      ALU.max))
                flat = lambda a: a.rearrange("p a t -> p (a t)")
                rsqrt(dve, flat(L), SS, 1024, flat(T1), flat(T2))
                link(dve, nc.vector.tensor_tensor(KK, KK, L, ALU.mult))
                dve.wait_ge(Sx("lrd"), 6)
                link(dve, nc.vector.tensor_scalar(LD, LD, 1.0, -0.5 * LAM, ALU.add, ALU.mult))
                link(dve, nc.vector.tensor_scalar(A, A, 0.5, 0.5, ALU.mult, ALU.add))
                for i in range(4):
                    link(dve, nc.vector.tensor_tensor_scan(out=L[:, i, :], data0=SCANM, data1=LD[:, i, :], initial=0.0,
                                                           op0=ALU.mult, op1=ALU.add))
                nc.vector.tensor_tensor(LD, L, LD, ALU.subtract).then_inc(Sx("L"), 1)
                for i in range(4):
                    link(dve, nc.vector.tensor_scalar(T1[:, i, :], A[:, i, :], -1.0, v("k_a", i), ALU.add, ALU.mult))
                link(dve, nc.vector.scalar_tensor_tensor(K_, T1, 1.0, K_, ALU.add, ALU.mult))
                for i in range(4):
                    x = nc.vector.scalar_tensor_tensor(T1[:, i, :], R[:, i, :], v("r_k", i), K_[:, i, :],
                                                       ALU.mult, ALU.mult)
                x.then_inc(Sx("bon"), 1)
                link(dve, nc.vector.tensor_tensor(A, A, KK, ALU.mult))
                dve.wait_ge(Sx("e"), 3)
                pt = lambda a: a.rearrange("p h (t n) -> p h t n", n=P)
                for t in range(2):
                    ts_ = slice(t * P, (t + 1) * P)
                    x = nc.vector.tensor_tensor(ART[:, :, t, 1, :], R[:, :, ts_], E1[:, :, ts_], ALU.mult)
                x.then_inc(Sx("tld"), 1)
                link(dve, nc.vector.tensor_copy(EC, E1.rearrange("p h (c n) -> p h c n", n=C)[:, :, :, C - 1]))
                nc.vector.tensor_tensor(BT, A, E2, ALU.mult).then_inc(Sx("tld"), 1)
                nc.vector.tensor_tensor(KTt, K_, E2, ALU.mult).then_inc(Sx("tld"), 1)
                for t in range(2):
                    ts_ = slice(t * P, (t + 1) * P)
                    x = nc.vector.scalar_tensor_tensor(ART[:, :, t, 0, :], KK[:, :, ts_], -1.0, LD[:, :, ts_],
                                                       ALU.mult, ALU.mult)
                x.then_inc(Sx("tld"), 1)
                dve.wait_ge(Sx("bs"), 1)
                for i in range(4):
                    x = nc.vector.tensor_tensor(V[:, i, :], V[:, i, :], acc[2 + i // 2][:, (i % 2) * T:(i % 2 + 1) * T],
                                                ALU.mult)
                x.then_inc(Sx("bvd"), 1)
                ub = [acc[2], acc[3], pj[2], mb]
                dve.wait_ge(Sx("tld"), 4)
                dve.wait_ge(Sx("masks"), 32)
                for u in range(16):
                    dve.wait_ge(Sx("ap"), u + 1)
                    nc.vector.tensor_tensor(AM[:, u].rearrange("p a n -> p (a n)"), ub[u % 4][:, :], AMASK, ALU.mult)\
                        .then_inc(Sx("am"), 1)
                dve.wait_ge(Sx("wy"), 2)
                for x_, banks in ((W1, (acc[0], acc[1])), (YP, (pj[0], pj[1]))):
                    for t in range(2):
                        nc.vector.tensor_copy(x_[:, t, :], banks[t][:, :]).then_inc(Sx("wyc"), 1)
                dve.wait_ge(Sx("am"), 16)
                for g in range(4):
                    nc.vector.tensor_copy(Z[:, 4 * g:4 * g + 4, :], ident[:, None, :].to_broadcast([P, 4, P]))\
                        .then_inc(Sx("zi"), 1)
                    nc.vector.tensor_copy(ZT[g], ident[:, None, :].to_broadcast([P, 4, P])).then_inc(Sx("zt"), 1)
                zb = [acc[2], acc[3], pj[2], mb]
                dve.wait_ge(Sx("zi"), 4)
                for lv in range(6):
                    for g in range(4):
                        us = slice(4 * g, 4 * g + 4)
                        if lv == 0:
                            nc.vector.tensor_tensor(AM[:, us, 2, :], AM[:, us, 0, :],
                                                    LEV[:, lv, None, :].to_broadcast([P, 4, P]), ALU.mult)\
                                .then_inc(Sx("E"), 1)
                    for g in range(4):
                        us = slice(4 * g, 4 * g + 4)
                        dve.wait_ge(Sx("Zp"), 4 * lv + g + 1)
                        if lv < 5:
                            dve.wait_ge(Sx("ZTp"), 4 * lv + g + 1)
                        nc.vector.tensor_tensor(Z[:, us, :], Z[:, us, :],
                                                u4((acc[0], acc[1], pj[0], pj[1])[g]), ALU.add).then_inc(Sx("zn"), 1)
                        if lv < 5:
                            nc.vector.tensor_tensor(ZT[g], ZT[g], u4(zb[g]), ALU.add).then_inc(Sx("zt"), 1)
                            nc.vector.tensor_tensor(AM[:, us, 2, :], AM[:, us, 0, :],
                                                    LEV[:, lv + 1, None, :].to_broadcast([P, 4, P]), ALU.mult)\
                                .then_inc(Sx("E"), 1)
                    dve.wait_ge(Sx("zn"), 4 * lv + 4)
                    if lv < 5:
                        dve.wait_ge(Sx("zt"), 4 * lv + 8)
                        dve.wait_ge(Sx("E"), 4 * lv + 8)
                Uv = lambda t: AM[:, 4 * t:4 * t + 4, 2, :]
                for c in range(4):
                    t, half = divmod(c, 2)
                    cr = slice(64 * half, 64 * half + 64)
                    if c:
                        dve.wait_ge(Sx("x"), c)
                        for odd in range(2):
                            hv = lambda a: a.rearrange("p (a b n) -> p a b n", b=2, n=C)[:, :, odd, :]
                            x = nc.vector.tensor_tensor(hv(X1[cr, :]), acc[odd][cr, 0:4 * C].rearrange(
                                "p (a n) -> p a n", n=C), hv(W1[cr, t, :]), ALU.add)
                        x.then_inc(Sx("X"), 1)
                    dve.wait_ge(Sx("up"), c + 1)
                    nc.vector.tensor_copy(Uv(t)[cr], acc[2][cr, :].rearrange("p (a n) -> p a n", n=P))\
                        .then_inc(Sx("U"), 1)
                    if c < 3:
                        dve.wait_ge(Sx("sp"), c + 1)
                        src = acc[3][:, 0:4 * C].rearrange("p (a n) -> p a n", n=C)
                        if c:
                            link(dve, nc.vector.tensor_tensor(ST[:, c, :, :], src, ST[:, c - 1, :, :], ALU.add))
                            src = ST[:, c, :, :]
                        nc.vector.tensor_tensor(ST[:, c, :, :], src, EC[:, :, c:c + 1].to_broadcast([P, 4, C]),
                                                ALU.mult).then_inc(Sx("S"), 1)
                        dve.wait_ge(Sx("S"), c + 1)
                dve.wait_ge(Sx("y2"), 1)
                yb = [pj[0], pj[1], pj[2], mb]
                for t in range(2):
                    link(dve, nc.vector.tensor_tensor(YP[:, t, :], YP[:, t, :], acc[t][:, :], ALU.add))
                for t in range(2):
                    rr = slice(64, 128) if t == 0 else slice(0, 128)
                    for odd in range(2):
                        hv = lambda a: a.rearrange("p (a b n) -> p a b n", b=2, n=C)[:, :, odd, :]
                        link(dve, nc.vector.tensor_tensor(hv(YP[rr, t, :]), hv(YP[rr, t, :]),
                                                          yb[2 * t + odd][rr, 0:4 * C].rearrange("p (a n) -> p a n", n=C),
                                                          ALU.add))
                group_norm(dve, YP.rearrange("p t (h n) -> p (t h) n", n=C), C,
                           W1.rearrange("p t (h n) -> p (t h) n", n=C), rw_stat, 64e-5).then_inc(Sx("ygn"), 1)
                dve.wait_ge(Sx("yt"), 1)
                for i in range(4):
                    Y = YF[:, i, :]
                    link(dve, nc.vector.tensor_scalar(Y, acc[2 + i // 2][:, (i % 2) * T:(i % 2 + 1) * T], v("ln_g", i),
                                                      v("ln_b", i), ALU.mult, ALU.add))
                    link(dve, nc.vector.tensor_tensor(Y, Y, V[:, i, :], ALU.add))
                    nc.vector.tensor_tensor(Y, Y, G[:, i, :], ALU.mult).then_inc(Sx("yf"), 1)
                for i in range(4):
                    dve.wait_ge(Sx("rhi"), 5 + i)
                    nc.vector.tensor_tensor(AR[:, 8 + i, :], YF[:, i, :], AR[:, i, :].bitcast(F32), ALU.subtract)\
                        .then_inc(Sx("rdy"), 1)
                w.g += 4

            def act_f(act, w):
                for c in range(15):
                    act_phase(act, w, 1, is_proj=True)
                act.wait_ge(pj_free, 3 + w.p)
                fl = lambda a: a.rearrange("p a t -> p (a t)")
                nc.scalar.activation(fl(TG), fl(RG), ACT.Tanh, scale=0.5).then_inc(Sx("tg"), 1)
                nc.scalar.activation(XWG[:, 1, :], XWG[:, 1, :], ACT.Tanh, scale=0.5).then_inc(Sx("sxg"), 1)
                nc.scalar.activation(XWG[0:64, 0, :], XWG[0:64, 0, :], ACT.Tanh).then_inc(Sx("lin"), 2)
                for h in range(4):
                    act.wait_ge(Sx("rend"), h + 1)
                    nc.scalar.activation(AR[:, 4 + h, :], O2[:, h // 2, (h % 2) * T:(h % 2 + 1) * T], ACT.Copy)\
                        .then_inc(Sx("rhi"), 1)
                act.dma_start(AMASK, c_dram("amask")).then_inc(Sx("masks"), 16)
                act.dma_start(LEV.rearrange("p a n -> p (a n)"), c_dram("levels")).then_inc(Sx("masks"), 16)
                act.wait_ge(Sx("kk"), 4)
                nc.scalar.activation(KS, KK, ACT.Square).then_inc(Sx("kks"), 1)
                act.wait_ge(Sx("h0"), 1)
                act.wait_ge(Sx("lr"), 1)
                for dst, banks, off in ((LD, (pj[0], pj[1]), HW0), (A, (acc[0], acc[1]), HA0)):
                    for i in range(4):
                        x = nc.scalar.activation(dst[:, i, :], banks[i // 2][:, (i % 2) * T:(i % 2 + 1) * T], ACT.Tanh,
                                                 scale=0.5, bias=off[:, i:i + 1])
                    x.then_inc(Sx("lrd"), 2)
                for b in range(2):
                    nc.scalar.activation(fl(G[:, 2 * b:2 * b + 2, :]), acc[2 + b][:, :], ACT.Copy)\
                        .then_inc(Sx("lrd"), 1)
                for t in range(2):
                    act.wait_ge(Sx("vt"), t + 1)
                    nc.scalar.activation(TM[:, 2, t, :], acc[t][:, :], ACT.Copy).then_inc(Sx("vtc"), 1)
                act.wait_ge(Sx("L"), 1)
                nc.scalar.activation(fl(E1), fl(L), ACT.Exp).then_inc(Sx("e"), 1)
                nc.scalar.activation(fl(E2), fl(L), ACT.Exp, scale=-1.0).then_inc(Sx("e"), 1)
                nc.scalar.activation(fl(LD), fl(LD), ACT.Exp).then_inc(Sx("e"), 1)
                for n in range(4):
                    x, t = divmod(n, 2)
                    act.wait_ge(Sx("tt"), n + 1)
                    nc.scalar.activation(TM[:, x, t, :], (acc[0], acc[1], pj[0], pj[1])[n][:, :], ACT.Copy)\
                        .then_inc(Sx("ttc"), 1)
                zb = [acc[2], acc[3], pj[2], mb]
                for lv in range(6):
                    for g in range(4):
                        act.wait_ge(Sx("Qp"), 4 * lv + g + 1)
                        nc.scalar.activation(AM[:, 4 * g:4 * g + 4, 3, :], u4(zb[g]), ACT.Copy).then_inc(Sx("Q"), 1)
                for i in range(4):
                    act.wait_ge(Sx("yf"), i + 1)
                    nc.scalar.activation(AR[:, i, :], YF[:, i, :], ACT.Copy).then_inc(Sx("rhi"), 1)
                out_act(act, w, 8)

            def load(act):
                for dst, src in ((DEC.rearrange("p a n -> p (a n)"), c_dram("decay")), (ROC, c_dram("rot_c")),
                                 (ROS, c_dram("rot_s")), (SCANM, c_dram("scan")), (SWP, c_dram("swap"))):
                    act.dma_start(dst, src).then_inc(Sx("ld"), 16)
                act.dma_start(WA2, small[:, SCOL["wa2"][0]:SCOL["wa2"][0] + 512]).then_inc(Sx("ld"), 16)
                act.dma_start(G2, small[:, SCOL["g2"][0]:SCOL["g2"][0] + 512]).then_inc(Sx("ld"), 16)
            return pe_f, dve_f, act_f, load

        from_stage = {"ffn": lambda tag, k: ffn(tag), "na": mixer, "dil": mixer, "xa": xattn, "dsa": dsa, "rwrt": rwrt}

        plan = []
        for s, (kind, idx) in enumerate(stages):
            fns = from_stage[kind](f"s{s}", kind)
            plan.append((s, kind, idx, fns))

        block = ctx.enter_context(nc.Block())

        def half_of(kind, idx):
            return 0.5 if kind == "ffn" and idx >= 2 else 1.0

        @block.sync
        def _(sp):
            for k in range(KT):
                sp.dma_start(xT[:, k, :], xin[:, k, :]).then_inc(loaded, 16)
            sp.dma_start(vecs[:, :], vecs_d).then_inc(loaded, 16)
            sp.dma_start(cst[:, 0:384], consts_d[:, 0:384]).then_inc(loaded, 16)
            sp.dma_start(cst[:, 384:400], c_dram("slopes")).then_inc(loaded, 16)
            for j in range(3):
                sp.dma_start(raw[:, j, :], wstream[j, :, :]).then_inc(w_raw[j], 16)
            with sp.Fori(1, NCH // 3) as i:
                for j in range(3):
                    sp.wait_ge(w_lo, i * 3 + (j - 2))
                    sp.dma_start(raw[:, j:j + 1, :], wstream[bass.ds(i * 3 + j, 1), :, :].rearrange("a p n -> p a n"))\
                        .then_inc(w_raw[j], 16)
            for g in range(NCH // 3 * 3, NCH):
                sp.wait_ge(w_lo, g - 2)
                sp.dma_start(raw[:, g % 3, :], wstream[g, :, :]).then_inc(w_raw[g % 3], 16)
            sp.wait_ge(*at("end", "x", KT))
            for k in range(KT):
                sp.dma_start(out[:, k, :], xT[:, k, :]).then_inc(sem("stored"), 16)
            sp.wait_ge(sem("stored"), 16 * KT)

        @block.gpsimd
        def _(gp):
            def low(g, s):
                gp.wait_ge(w_hi, g + 1)
                nc.gpsimd.tensor_tensor(wlo[:, s, :], raw[:, s, :], whi[:, s, :].bitcast(F32),
                                        ALU.subtract).then_inc(w_lo, 1)
            with gp.Fori(0, NCH // 3) as i:
                for j in range(3):
                    low(i * 3 + j, j)
            for g in range(NCH // 3 * 3, NCH):
                low(g, g % 3)

        @block.scalar
        def _(act):
            w = Walk()
            act.wait_ge(loaded, 16 * (KT + 3))
            for s, kind, idx, fns in plan:
                if len(fns) > 3 and s == 0:
                    fns[3](act)
            pre_act(act, "s0pre", f"{plan[0][1]}{plan[0][2]}_pre", plan[0][1] == "dil")
            for j in range(3):
                act.wait_ge(w_raw[j], 16)
                nc.scalar.activation(whi[:, j, :], raw[:, j, :], ACT.Copy).then_inc(w_hi, 1)
            for s, kind, idx, fns in plan:
                fns[2](act, w)
                post_act(act, w, f"s{s}post")
                if s + 1 < len(plan):
                    nx = plan[s + 1]
                    pre_act(act, f"s{s + 1}pre", f"{nx[1]}{nx[2]}_pre", nx[1] == "dil")
                    if len(nx[3]) > 3:
                        nx[3][3](act)

        @block.vector
        def _(dve):
            w = Walk()
            nc.vector.memset(nt[:, :], 0.0).then_inc(pj_free, 3)
            dve.wait_ge(pj_free, 3)
            dve.wait_ge(loaded, 16 * (KT + 3))
            pre_dve(dve, "s0pre", f"{plan[0][1]}{plan[0][2]}_pre", plan[0][1] == "dil")
            for s, kind, idx, fns in plan:
                fns[1](dve, w)
                if s + 1 < len(plan):
                    nx = plan[s + 1]
                    nxt = (f"s{s + 1}pre", f"{nx[1]}{nx[2]}_pre", nx[1] == "dil")
                else:
                    nxt = ("end", None, False)
                post_dve(dve, f"s{s}post", f"{kind}{idx}_post", half_of(kind, idx), nxt)
                if s + 1 < len(plan):
                    pre_dve(dve, *nxt, done_lo=True)

        @block.tensor
        def _(pe):
            w = Walk()
            pe.wait_ge(loaded, 16 * (KT + 3))
            pre_pe(pe, "s0pre")
            for s, kind, idx, fns in plan:
                fns[0](pe, w)
                post_pe(pe, f"s{s}post")
                if s + 1 < len(plan):
                    pre_pe(pe, f"s{s + 1}pre")


def extra_tiles(kind, idx, w):
    if kind == "xa":
        return [fm_tile(w[n][idx], h * P) for n in ("xa_wq_2", "xa_wk_2", "xa_wv_2") for h in range(4)]
    if kind == "rwrt":
        W = w["ev_w_in_2"][0]
        rt = [1792 + 512 * i + P * h for i in range(4) for h in range(4)]
        return [fm_tile(W, c) for c in rt + [P * i for i in range(14)]]
    W = w["od_w_in_2"][0]
    pad = lambda a: np.concatenate([a, np.zeros((D, P - a.shape[1]), np.float32)], axis=1)
    kidx = W[:, 384:448]
    return ([fm_tile(W, 0), fm_tile(W, P), fm_tile(W, 2 * P), fm_tile(np.concatenate([kidx, kidx], axis=1), 0),
             fm_tile(pad(W[:, 448:456]), 0)] + [fm_tile(W, 456 + i * P) for i in range(12)]
            + [np.zeros((P, D), np.float32)])


def fm_tile(W, c):
    return W[:, c:c + P].reshape(KT, P, P).transpose(1, 0, 2).reshape(P, KT * P)


def stage_tiles(kind, idx, w):
    if kind == "ffn":
        wg, wu, _ = ffn_weights(idx, w)
        return [x for j in range(FT) for x in (fm_tile(wg, j * P), fm_tile(wu, j * P))]
    if kind == "na":
        W = w["na_w_qkv"][0]
        return [fm_tile(W, i * D + hp * P) for hp in range(8) for i in range(3)]
    if kind == "dil":
        W = w["dil_w_qkv"][0]
        return [fm_tile(W, g * 3 * D + i * D + hp * P) for hp in range(8) for g in range(3) for i in range(3)]
    return extra_tiles(kind, idx, w)


def ffn_weights(idx, w):
    if idx < 2:
        return w["ffn_w_gate"][idx], w["ffn_w_up"][idx], w["ffn_w_down"][idx]
    l, j = divmod(idx - 2, 2)
    return w["ffn_w_gate_2"][l, j], w["ffn_w_up_2"][l, j], w["ffn_w_down_2"][l, j]


def out_weight(kind, idx, w):
    if kind == "ffn":
        return ffn_weights(idx, w)[2]
    return {"na": w["na_w_o"][0], "dil": w["dil_w_o"][0], "rwrt": w["ev_w_out_2"][0], "dsa": w["od_w_out_2"][0],
            "xa": w["xa_wo_2"][idx if kind == "xa" else 0]}[kind]


def host_arrays(stages, w):
    chunks = []
    for kind, idx in stages:
        t = stage_tiles(kind, idx, w)
        assert len(t) == 2 * proj_chunks(kind), (kind, len(t))
        chunks += [np.concatenate(t[i:i + 2], axis=1) for i in range(0, len(t), 2)]
        W = out_weight(kind, idx, w)
        chunks += [np.concatenate([W[i:i + P], W[i + P:i + 2 * P]], axis=1) for i in range(0, len(W), 2 * P)]
    stream = np.stack(chunks)
    cols = lambda a: np.ascontiguousarray(np.asarray(a).reshape(-1, P).T)
    gains = {}
    for kind, idx in STAGES:
        if kind == "ffn" and idx < 2:
            a = (w["norm_ffn_pre"][idx], w["norm_ffn_post"][idx])
        elif kind in ("na", "dil"):
            i = 0 if kind == "na" else 1
            a = (w["norm_mix_pre"][i], w["norm_mix_post"][i])
        else:
            l, j = {("ffn", 2): (0, 0), ("rwrt", 0): (0, 2), ("xa", 0): (0, 4), ("ffn", 3): (0, 6),
                    ("ffn", 4): (1, 0), ("dsa", 0): (1, 2), ("xa", 1): (1, 4), ("ffn", 5): (1, 6)}[kind, idx]
            a = (w["norm_g_2"][l, j], w["norm_g_2"][l, j + 1])
        gains[f"{kind}{idx}_pre"], gains[f"{kind}{idx}_post"] = a
    gains.update(mem_g=w["mem_norm_g_2"], mu=w["rw_mu_2"][0], w0=w["rw_w0_2"][0], a0=w["rw_a0_2"][0],
                 k_k=w["rw_k_k_2"][0], k_a=w["rw_k_a_2"][0], r_k=w["rw_r_k_2"][0], ln_g=w["rw_ln_g_2"][0],
                 ln_b=w["rw_ln_b_2"][0], gn_g=w["rt_gn_g_2"][0], gn_b=w["rt_gn_b_2"][0],
                 qn=w["dsa_q_norm_g_2"][0], kvn=w["dsa_kv_norm_g_2"][0], cw0=w["sc_conv_w_2"][0, 0],
                 cw1=w["sc_conv_w_2"][0, 1], cw2=w["sc_conv_w_2"][0, 2], cb=w["sc_conv_b_2"][0])
    vec = np.concatenate([cols(gains[n]) for n, _ in VECS], axis=1)
    fm = lambda a: np.ascontiguousarray(a.T.reshape(KT, P, T).transpose(1, 0, 2))
    small = small_weights(w)
    return dict(wstream=stream, xin=fm(w["x"][0]), memin=fm(w["mem_2"][0]), vecs=vec, consts=const_tables(),
                rpb=shifted_rows(w["na_rpb"][0].reshape(-1)), small=small)


def shifted_rows(a):
    p_ = np.concatenate([np.zeros(63, np.float32), a])
    return np.stack([p_[63 - q:63 - q + len(a)] for q in range(64)])


def const_tables():
    f = np.float32
    i = np.arange(P)
    c = {"ident": np.eye(P), "ones": np.ones((P, P)), "blk": (i[:, None] // 64 == i[None] // 64) * 1.0,
         "swap": ((i[:, None] + 64) % P == i[None]) * 1.0,
         "slopes": np.broadcast_to(-(2.0 ** (-8.0 * np.arange(1, HEADS + 1) / HEADS)), (P, HEADS))}
    q, k = i % 64, np.arange(64)
    start = np.clip(q - 8, 0, 48)
    c["na_mask"] = np.where((k[None] >= start[:, None]) & (k[None] < start[:, None] + 16), 0.0, -1e30)
    pos = np.arange(T)
    tok = (pos % 64) * 4 + pos // 64
    dist = np.zeros((P, 2, 512))
    for t in range(2):
        tq = tok[t * P:(t + 1) * P]
        d = np.abs(tq[:, None] - tok[None])
        own = d[:, t * P:(t + 1) * P]
        same = lambda m: (tq[:, None] - tq[None]) % m == 0
        dist[:, t, :T] = np.where(d <= 64, d, 1e32)
        dist[:, t, T:T + P] = np.where(same(4), own, 1e32)
        dist[:, t, T + P:] = np.where(same(16), own, 1e32)
    c["dist"] = dist.reshape(P, -1)
    inv = 10000.0 ** (-np.arange(64) / 64.0)
    ang = (pos[None].astype(f) * inv.astype(f)[:, None]).astype(f).astype(np.float64)
    c["rot_c"] = np.cos(np.concatenate([ang, ang]))
    c["rot_s"] = np.concatenate([-np.sin(ang), np.sin(ang)])
    dec = np.zeros((P, RT_H, 2, T))
    for h in range(RT_H):
        for st in range(2):
            rel = pos[None] - (st * P + i)[:, None]
            dec[:, h, st] = np.where(rel >= 0, (1 - 2.0 ** (-5.0 - h)) ** np.maximum(rel, 0), 0)
    c["decay"] = dec.reshape(P, -1)
    same = i[:, None] // 64 == i[None] // 64
    strict, incl = same & (i[:, None] < i[None]), same & (i[:, None] <= i[None])
    c["amask"] = np.concatenate([strict, incl, strict, incl], axis=1)
    c["levels"] = np.concatenate([(i[:, None] // (2 * s) == i[None] // (2 * s)) & (i[:, None] % (2 * s) < s)
                                  & (i[None] % (2 * s) >= s) for s in (1, 2, 4, 8, 16, 32)], axis=1)
    c["scan"] = np.broadcast_to(pos % 64 != 0, (P, T))
    c["causal"] = np.concatenate([np.where(pos[None] <= (t * P + i)[:, None], 0.0, -1e30) for t in range(2)], axis=1)
    return np.concatenate([np.asarray(c[n], f) for n, _ in CONSTS], axis=1)


def small_weights(w):
    s = np.zeros((P, SMALL_N), np.float32)
    for name, a in small_parts(w).items():
        at, n = SCOL[name]
        s[:, at:at + n] = a
    return s


def kernel(**inputs):
    import concourse.bacc as bacc
    from concourse.bass_utils import run_bass_kernel_spmd

    w = {n: np.asarray(a) for n, a in inputs.items()}
    arrays = host_arrays(STAGES, w)
    nc = bacc.Bacc("TRN2", target_bir_lowering=False, num_devices=1)
    aps = {n: nc.dram_tensor("in_" + n, a.shape, mybir.dt.from_np(a.dtype), kind="ExternalInput").ap()
           for n, a in arrays.items()}
    out = nc.dram_tensor("out", (P, KT, T), F32, kind="ExternalOutput").ap()
    build_program(nc, STAGES, aps["wstream"], aps["xin"], aps["memin"], aps["vecs"], aps["consts"], aps["rpb"],
                  aps["small"], out)
    r = run_bass_kernel_spmd(nc, [{"in_" + n: a for n, a in arrays.items()}], core_ids=[0])
    y = r.results[0]["out"]
    return np.ascontiguousarray(y.transpose(1, 0, 2).reshape(D, T).T)[None]
```
